# Optimizing a Trainium2 kernel written in Bass

```python
import jax, jax.numpy as jnp
from jax import lax
import numpy as np

D_MODEL = 1024
BATCH = 1
SEQ = 512
DEPTH = 1
DEC_BATCH = 8
DEC_SEQ = 1
PAST_LEN = 4096
PAGE_SIZE = 128

D_A = D_MODEL
D_B = D_MODEL
N_MEM = 256
N_XHEADS = 4
D_XHEAD = D_MODEL // N_XHEADS
D_X = N_XHEADS * D_XHEAD
N_BRANCH = 3
K_A = 3
K_B = 31
D_FF = -(-8 * D_MODEL // (3 * 256)) * 256
SPLIT_SIZES = (D_A, D_A, D_A, D_B, D_B, D_X, N_BRANCH * D_MODEL)
D_IN = sum(SPLIT_SIZES)
EPS = 1e-6

kernel_name = "gated_branch_conv_xattn_decoder_step"

def rmsnorm(x, g):
    x32 = x.astype(jnp.float32)
    y = x32 * lax.rsqrt(jnp.mean(x32 * x32, axis=-1, keepdims=True) + EPS)
    return y.astype(x.dtype) * g

def layernorm(x, g, b):
    x32 = x.astype(jnp.float32)
    mu = jnp.mean(x32, axis=-1, keepdims=True)
    var = jnp.mean(jnp.square(x32 - mu), axis=-1, keepdims=True)
    y = (x32 - mu) * lax.rsqrt(var + EPS)
    return y.astype(x.dtype) * g + b

def causal_dwconv(buf, u, w):
    seq = jnp.concatenate([buf.astype(u.dtype), u], axis=1)
    taps = w.shape[0]
    out = lax.conv_general_dilated(
        seq, w.astype(seq.dtype)[:, None, :], window_strides=(1,), padding="VALID",
        dimension_numbers=("NWC", "WIO", "NWC"), feature_group_count=u.shape[-1])
    return out, seq[:, seq.shape[1] - (taps - 1):, :]

def mem_kv(mem, norm_mem, w_k, w_v):
    m = rmsnorm(mem, norm_mem)
    k = jnp.einsum("bmd,dhe->bmhe", m, w_k)
    v = jnp.einsum("bmd,dhe->bmhe", m, w_v)
    return k, v

def layer(x, buf_a, buf_b, mem_k, mem_v, norm_mix, w_in, b_gate, conv_a_w, w_out_a,
          conv_b_w, conv_b_bias, ln_b_g, ln_b_b, w_out_b, w_out_x, w_o,
          norm_ffn, w_ff_gate, w_ff_up, w_ff_down):
    bsz, t, _ = x.shape
    xn = rmsnorm(x, norm_mix)
    proj = xn @ w_in
    cuts = [int(c) for c in np.cumsum(SPLIT_SIZES)[:-1]]
    a_b, a_c, a_x, b_val, b_glu, q, gate_logits = jnp.split(proj, cuts, axis=-1)

    ya, new_a = causal_dwconv(buf_a, a_c * a_x, conv_a_w)
    ya = (a_b * ya) @ w_out_a

    ub = b_val * jax.nn.sigmoid(b_glu)
    yb, new_b = causal_dwconv(buf_b, ub, conv_b_w)
    yb = jax.nn.silu(layernorm(yb + conv_b_bias, ln_b_g, ln_b_b)) @ w_out_b

    qh = q.reshape(bsz, t, N_XHEADS, D_XHEAD)
    s = jnp.einsum("bthe,bmhe->bhtm", qh, mem_k.astype(qh.dtype)).astype(jnp.float32)
    p = jax.nn.softmax(s * (D_XHEAD ** -0.5), axis=-1).astype(x.dtype)
    o = jnp.einsum("bhtm,bmhe->bthe", p, mem_v.astype(x.dtype)).reshape(bsz, t, D_X)
    yx = o @ w_out_x

    g = jax.nn.sigmoid(gate_logits + b_gate).reshape(bsz, t, N_BRANCH, D_MODEL)
    merged = g[:, :, 0] * ya + g[:, :, 1] * yb + g[:, :, 2] * yx
    h = x + merged @ w_o

    hn = rmsnorm(h, norm_ffn)
    h = h + (jax.nn.silu(hn @ w_ff_gate) * (hn @ w_ff_up)) @ w_ff_down
    return h, new_a, new_b

def setup_inputs(seed: int = 0) -> dict:
    key = jax.random.key(seed)
    ks = jax.random.split(key, 32)
    f32 = jnp.float32

    def nrm(k, shape, scale):
        return jax.random.normal(k, shape, f32) * scale

    def gain(k, shape):
        return 1.0 + 0.05 * jax.random.normal(k, shape, f32)

    L = DEPTH
    return {
        "x_prompt": nrm(ks[0], (BATCH, SEQ, D_MODEL), 1.0),
        "x_sample": nrm(ks[1], (DEC_BATCH, DEC_SEQ, D_MODEL), 1.0),
        "mem_prompt": nrm(ks[2], (BATCH, N_MEM, D_MODEL), 1.0),
        "cache_mem_k": nrm(ks[3], (L, DEC_BATCH, N_MEM, N_XHEADS, D_XHEAD), 1.0),
        "cache_mem_v": nrm(ks[4], (L, DEC_BATCH, N_MEM, N_XHEADS, D_XHEAD), 1.0),
        "state_conv_a": nrm(ks[5], (L, DEC_BATCH, K_A - 1, D_A), 1.0),
        "state_conv_b": nrm(ks[6], (L, DEC_BATCH, K_B - 1, D_B), 1.0),
        "norm_mix": gain(ks[7], (L, D_MODEL)),
        "w_in": nrm(ks[8], (L, D_MODEL, D_IN), D_MODEL ** -0.5),
        "b_gate": nrm(ks[9], (L, N_BRANCH * D_MODEL), 0.1),
        "conv_a_w": nrm(ks[10], (L, K_A, D_A), K_A ** -0.5),
        "w_out_a": nrm(ks[11], (L, D_A, D_MODEL), D_A ** -0.5),
        "conv_b_w": nrm(ks[12], (L, K_B, D_B), K_B ** -0.5),
        "conv_b_bias": nrm(ks[13], (L, D_B), 0.1),
        "ln_b_g": gain(ks[14], (L, D_B)),
        "ln_b_b": nrm(ks[15], (L, D_B), 0.1),
        "w_out_b": nrm(ks[16], (L, D_B, D_MODEL), D_B ** -0.5),
        "norm_mem": gain(ks[17], (L, D_MODEL)),
        "w_k": nrm(ks[18], (L, D_MODEL, N_XHEADS, D_XHEAD), D_MODEL ** -0.5),
        "w_v": nrm(ks[19], (L, D_MODEL, N_XHEADS, D_XHEAD), D_MODEL ** -0.5),
        "w_out_x": nrm(ks[20], (L, D_X, D_MODEL), D_X ** -0.5),
        "w_o": nrm(ks[21], (L, D_MODEL, D_MODEL), D_MODEL ** -0.5),
        "norm_ffn": gain(ks[22], (L, D_MODEL)),
        "w_ff_gate": nrm(ks[23], (L, D_MODEL, D_FF), D_MODEL ** -0.5),
        "w_ff_up": nrm(ks[24], (L, D_MODEL, D_FF), D_MODEL ** -0.5),
        "w_ff_down": nrm(ks[25], (L, D_FF, D_MODEL), D_FF ** -0.5),
        "norm_final": gain(ks[26], (D_MODEL,)),
    }

def reference(x_prompt, x_sample, mem_prompt, cache_mem_k, cache_mem_v, state_conv_a,
              state_conv_b, norm_mix, w_in, b_gate, conv_a_w, w_out_a, conv_b_w,
              conv_b_bias, ln_b_g, ln_b_b, w_out_b, norm_mem, w_k, w_v, w_out_x, w_o,
              norm_ffn, w_ff_gate, w_ff_up, w_ff_down, norm_final):
    hp, hs = x_prompt, x_sample
    bp = x_prompt.shape[0]
    mk_p, mv_p, ca_p, cb_p, ca_s, cb_s = [], [], [], [], [], []
    for l in range(DEPTH):
        lp = (norm_mix[l], w_in[l], b_gate[l], conv_a_w[l], w_out_a[l], conv_b_w[l],
              conv_b_bias[l], ln_b_g[l], ln_b_b[l], w_out_b[l], w_out_x[l], w_o[l],
              norm_ffn[l], w_ff_gate[l], w_ff_up[l], w_ff_down[l])
        k_p, v_p = mem_kv(mem_prompt, norm_mem[l], w_k[l], w_v[l])
        zero_a = jnp.zeros((bp, K_A - 1, D_A), hp.dtype)
        zero_b = jnp.zeros((bp, K_B - 1, D_B), hp.dtype)
        hp, na_p, nb_p = layer(hp, zero_a, zero_b, k_p, v_p, *lp)
        hs, na_s, nb_s = layer(hs, state_conv_a[l], state_conv_b[l],
                               cache_mem_k[l], cache_mem_v[l], *lp)
        mk_p.append(k_p); mv_p.append(v_p)
        ca_p.append(na_p); cb_p.append(nb_p)
        ca_s.append(na_s); cb_s.append(nb_s)
    y_prompt = rmsnorm(hp, norm_final)
    y_sample = rmsnorm(hs, norm_final)
    return (y_prompt, y_sample, jnp.stack(mk_p), jnp.stack(mv_p), jnp.stack(ca_p),
            jnp.stack(cb_p), jnp.stack(ca_s), jnp.stack(cb_s))


_drawn_inputs = setup_inputs


def setup_inputs(seed=0):
    import zlib

    import numpy as np

    out = dict(_drawn_inputs(seed))
    spreads = {}
    factors = {'ln_b_g': 3.178}
    for name, (base, spread) in spreads.items():
        noise = np.random.default_rng([zlib.crc32(name.encode()), seed]).standard_normal(out[name].shape)
        drawn = base * np.exp(spread * noise) if base else spread * noise
        out[name] = __import__('jax').numpy.asarray(drawn.astype(out[name].dtype))
    for name, factor in factors.items():
        out[name] = (out[name] * factor).astype(out[name].dtype)
    return out
```

```python
from contextlib import ExitStack

import numpy as np
import concourse.bass as bass
from concourse import mybir

P = 128
D = 1024
KT = D // P
TP, TS = 512, 8
TOK = TP + TS
HALF = TOK // 2
N_MEM, NH, DH = 256, 4, 256
K_A, K_B = 3, 31
D_FF = 2816
FT = D_FF // P
CW = 256
HK = KT // 2
EPS = 1e-6
PAD = K_B - 1
SLOT = PAD + TOK
SG = 2 + TOK

COL_AB, COL_AC, COL_AX, COL_BV, COL_BG, COL_Q, COL_GATE = (n * D for n in range(7))
BR_A, BR_B, BR_X = range(3)

(R_MEM, R_MIX, R_BG, R_CA, R_CB, R_CBIAS, R_LNG, R_LNB, R_FFN, R_ALL) = (
    0, 1, 2, 5, 8, 39, 40, 41, 42, 43)

C_KV, C_B, C_Q, C_CX, C_X, C_BA, C_A, C_GB, C_OB, C_WO, C_F, C_D, C_END = (
    0, 8, 16, 20, 28, 36, 40, 48, 52, 56, 60, 82, 94)


def number_uses():
    T, n = {}, 0

    def use(name, count=1):
        nonlocal n
        T[name] = n
        n += count

    use("param")
    use("mem", 2)
    for c in range(8):
        use(f"kv{c}")
        if 1 <= c <= NH:
            use(f"kt{c - 1}")
        use(f"prep{c}")
    use("b", 16)
    use("btail")
    for h in range(NH):
        use(f"q{h}", 2)
        if h:
            use(f"pt{h - 1}")
            use(f"qb{h - 1}", 2)
            use(f"o{h - 1}")
        use(f"qt{h}")
        use(f"s{h}")
    use("pt3")
    use("qb3", 2)
    use("o3")
    use("ss")
    use("sp")
    use("cx", 24)
    use("ctail")
    use("x", 16)
    use("ba", 8)
    use("a", 16)
    use("gb", 10)
    use("ob", 8)
    use("wo", 8)
    use("r")
    use("f", 2 * FT)
    for p in range(4):
        use(f"d{p}", 2)
        if p:
            use(f"y{p - 1}", 2)
    use("y3", 2)
    return T


def decoder_step(nc, x_prompt, x_sample, mem_prompt, cache_mem_k, cache_mem_v, state_conv_a,
                 state_conv_b, norm_mix, w_in, b_gate, conv_a_w, w_out_a, conv_b_w, conv_b_bias,
                 ln_b_g, ln_b_b, w_out_b, norm_mem, w_k, w_v, w_out_x, w_o, norm_ffn, w_ff_gate,
                 w_ff_up, w_ff_down, norm_final, y_prompt, y_sample, mem_k_out, mem_v_out,
                 conv_a_prompt, conv_b_prompt, conv_a_sample, conv_b_sample):
    f32, f32r = mybir.dt.float32, mybir.dt.float32r
    ALU, ACT, AX = mybir.AluOpType, mybir.ActivationFunctionType, mybir.AxisListType
    T = number_uses()

    def chunks(w):
        return w.rearrange("(k p) n -> p k n", p=P)

    win = chunks(w_in[0])
    wk = chunks(w_k[0].rearrange("d h e -> d (h e)"))
    wv = chunks(w_v[0].rearrange("d h e -> d (h e)"))
    woa, wob, wox, wo = (chunks(w[0]) for w in (w_out_a, w_out_b, w_out_x, w_o))
    wfg, wfu, wfd = (chunks(w[0]) for w in (w_ff_gate, w_ff_up, w_ff_down))
    kcache, vcache = (c[0].rearrange("s m h e -> (s m) (h e)").rearrange("(a p) c -> p a c", p=P)
                      for c in (cache_mem_k, cache_mem_v))
    kout, vout = (o[0, 0].rearrange("m h e -> m (h e)").rearrange("(t p) c -> p t c", p=P)
                  for o in (mem_k_out, mem_v_out))
    xs_dram = x_sample.rearrange("s t d -> (s t) d")
    sa_dram = state_conv_a[0].rearrange("s j d -> (s j) d")
    sb_dram = state_conv_b[0].rearrange("s j d -> (s j) d")
    SB_ROWS = TS * PAD // 2

    base = -(-nc.sbuf_base // 32) * 32
    used = {}

    def align(off):
        return -(-off // 32) * 32

    def at(name, shape, dt, off):
        size = 4 * int(np.prod(shape[1:]))
        used[name] = off + size
        return nc.alloc_sbuf_tensor_at(name, shape, dt, offset=base + off)

    CH_B = KT * CW * 4
    o_raw, o_wh, o_wl = 0, 2 * CH_B, 4 * CH_B
    o_bh = 6 * CH_B
    ACTV = KT * TOK
    BIG = 3 * ACTV
    o_bl = o_bh + 4 * BIG
    o_ub = o_bl + 4 * BIG
    o_mg = align(o_ub + 4 * (KT + 1) * SLOT)
    o_h = o_mg + 4 * ACTV
    o_sm = o_h + 4 * ACTV
    w_raw = at("w_raw", [P, 2, KT, CW], f32, o_raw)
    w_h = at("w_h", [P, 2, KT, CW], f32r, o_wh)
    w_l = at("w_l", [P, 2, KT, CW], f32r, o_wl)
    big_h = at("big_h", [P, BIG], f32r, o_bh)
    big_l = at("big_l", [P, BIG], f32r, o_bl)

    def part(big, n, words=ACTV, inner=TOK, skip=0):
        return big[:, n * ACTV + skip:n * ACTV + skip + words].rearrange("p (k t) -> p k t", t=inner)

    xn = [part(b, 0) for b in (big_h, big_l)]
    br = [part(b, 1) for b in (big_h, big_l)]
    zb = [part(b, 2) for b in (big_h, big_l)]
    mn = [part(b, 1, KT * N_MEM, N_MEM) for b in (big_h, big_l)]
    kT = [part(b, 2, KT * N_MEM, N_MEM) for b in (big_h, big_l)]
    vM = [part(b, 2, 2 * D, D, KT * N_MEM) for b in (big_h, big_l)]
    mid = [b[:, 0:FT * TOK].rearrange("p (k t) -> p k t", t=TOK) for b in (big_h, big_l)]
    mid_f = [b[:, 0:FT * TOK] for b in (big_h, big_l)]
    o_p2h, o_p2l = o_bh + 8 * ACTV, o_bl + 8 * ACTV
    x_st = at("x_st", [P, 4, D], f32, o_p2h)
    xs_st = at("xs_st", [TS, D], f32, o_p2l)
    hsum = at("hsum", [P, TOK], f32, o_p2l + 4 * D)
    tail = 4 * FT * TOK
    rms = at("rms", [P, TOK], f32, o_bh + tail)
    sgf = at("sgf", [P, 2, TOK], f32, o_bl + tail)
    ubyb = at("ubyb", [P, KT + 1, SLOT], f32, o_ub)
    merged = at("merged", [P, KT, TOK], f32, o_mg)
    yA = at("yA", [P, KT, TOK], f32, o_h)
    sgB = at("sgB", [P, KT, TOK], f32, o_h)
    h_sb = at("h_sb", [P, KT, TOK], f32, o_h)
    stage = [at(f"stage{n}", [P, D], f32, o_ub + 4 * D * n if n < 8 else o_h + 4 * D * (n - 6))
             for n in range(10)]
    prow = at("prow", [R_ALL, D], f32, o_h)
    kv_f = at("kv_f", [P, 2, 2, CW], f32, o_h + 4 * D)
    q_hl = [at(f"q_{n}", [P, 2, TOK], f32r, o_h + 8 * TOK * i) for i, n in enumerate("hl")]
    pt_hl = [at(f"pt_{n}", [P, 2, TP], f32r, o_h + 16 * TOK + 8 * TP * i) for i, n in enumerate("hl")]
    k_st = at("k_st", [P, 2 * TS, DH], f32, o_mg)
    v_st = at("v_st", [P, 2, TS, DH], f32, o_mg)
    uao = at("uao", [TS + 2, D], f32, o_mg + 4 * 6 * TOK)
    hg = [at(f"hg_{n}", [P, KT, TOK], f32r, o_ub + 4 * ACTV * i) for i, n in enumerate("hl")]
    y_st = at("y_st", [P, 4, D], f32, o_ub)
    ys_st = at("ys_st", [TS, D], f32, o_ub + 16 * D)
    gfin = at("gfin", [P, D], f32, o_ub + 20 * D)
    junk = at("junk", [P, D], f32, o_ub + 24 * D)
    o = o_sm
    sg = at("sg", [P, 2, SG], f32, o)
    p_f = at("p_f", [P, 4, N_MEM], f32, o)
    p32 = at("p32", [NH * TS, N_MEM], f32, o)
    nrm_t = at("nrm_t", [P, KT, P], f32, o)
    ubo = at("ubo", [PAD + TS, D], f32, o)
    o = align(o + 8 * SG)
    qs_hl = [at(f"qs_{n}", [TS, DH], f32r, o + 4 * DH * i) for i, n in enumerate("hl")]
    o += 8 * DH
    ident = at("ident", [P, P], f32, o)
    o += 4 * P
    prm = at("prm", [P, KT, R_ALL], f32, o)
    o += 4 * KT * R_ALL
    ysb = at("ysb", [P, KT, TS], f32, o)
    o += 4 * KT * TS
    ysa = at("ysa", [P, KT, TS], f32, o)
    o += 4 * KT * TS
    ua_tail = at("ua_tail", [P, KT, TS + 2], f32, o)
    o += 4 * KT * (TS + 2)
    qs_f = at("qs_f", [P, 2, TS], f32, o)
    o += 64
    sc = at("sc", [P, 2, NH * TS], f32, o)
    o += 256
    pT = at("pT", [P, 2, NH * TS], f32, o)
    o += 256
    ident_r = at("ident_r", [TS, TS], f32r, o)
    o += 32
    ones = at("ones", [P, 8], f32, o)
    eps = ones[:, 4:5]
    o += 32
    st = at("st", [P, 56], f32, o)
    o += 224
    ss, rs_, mx, nb, rsum, rrec = (st[:, a:b] for a, b in ((0, 8), (8, 16), (16, 20), (20, 24), (24, 28), (28, 32)))
    mx32, nb32, rsum32, rrec32 = (st[0:NH * TS, 32 + n:33 + n] for n in range(4))
    ssy, rfin = st[:, 36:46], st[:, 46:51]
    assert base + o <= nc.sbuf_usable_end, (base + o, nc.sbuf_usable_end)
    junk_norm = at("junk_norm", [P, D], f32, o_bh + 4 * (ACTV + KT * N_MEM))

    def flat(t):
        return t[:, :, :].rearrange("p a b -> p (a b)")

    prm_f, ubyb_f, merged_f, yA_f = flat(prm), flat(ubyb), flat(merged), flat(yA)

    def param(tile, row):
        if isinstance(tile, int):
            return prm[:, tile, row:row + 1]
        return prm_f[:, bass.ds(tile * R_ALL + row, 1)]

    ctx = ExitStack()
    with ctx:
        acc = [ctx.enter_context(nc.psum_tensor(f"acc{n}", [P, 2, 512], f32)) for n in range(4)]

        def sem(name):
            return ctx.enter_context(nc.semaphore(name))

        acc_done = sem("acc_done")
        acc_read = sem("acc_read")
        w_loaded = [sem("w_loaded0"), sem("w_loaded1")]
        w_hi = sem("w_hi")
        w_lo = sem("w_lo")
        row_in = [sem(f"row_in{n}") for n in range(10)]
        prow_in = sem("prow_in")
        const_made = sem("const_made")
        ident_made = sem("ident_made")
        stats_clear = sem("stats_clear")
        sumsq = sem("sumsq")
        meansq = sem("meansq")
        rootsq = sem("rootsq")
        row_scaled = sem("row_scaled")
        nrm_hi = sem("nrm_hi")
        nrm_lo = sem("nrm_lo")
        kv_hi = sem("kv_hi")
        kv_lo = sem("kv_lo")
        kv_stored = [sem("kv_stored0"), sem("kv_stored1")]
        state_sum = sem("state_sum")
        pads = sem("pads")
        b_sig = sem("b_sig")
        ubo_stored = sem("ubo_stored")
        q_hi = sem("q_hi")
        at_hi = sem("at_hi")
        at_exp = sem("at_exp")
        at_max = sem("at_max")
        at_step = sem("at_step")
        k_loaded = sem("k_loaded")
        v_loaded = [sem("v_loaded0"), sem("v_loaded1")]
        ss_max = sem("ss_max")
        ss_exp = sem("ss_exp")
        ss_step = sem("ss_step")
        cv_step = sem("cv_step")
        c_copied = sem("c_copied")
        u_used = sem("u_used")
        ca_step = sem("ca_step")
        v_hi = sem("v_hi")
        uao_stored = sem("uao_stored")
        x_sig = sem("x_sig")
        ba_hi = sem("ba_hi")
        ba_lo = sem("ba_lo")
        a_sig = sem("a_sig")
        a_step = sem("a_step")
        gb_sig = sem("gb_sig")
        ln_step = sem("ln_step")
        ln_sub = sem("ln_sub")
        ln_sq = sem("ln_sq")
        ln_acc = sem("ln_acc")
        ln_root = sem("ln_root")
        z_aff = sem("z_aff")
        z_sig = sem("z_sig")
        z_f = sem("z_f")
        z_hi = sem("z_hi")
        z_lo = sem("z_lo")
        m_sum = sem("m_sum")
        m_hi = sem("m_hi")
        m_lo = sem("m_lo")
        x_again = sem("x_again")
        h_hi = sem("h_hi")
        h_sq = sem("h_sq")
        h_sum = sem("h_sum")
        r_root = sem("r_root")
        f_sig = sem("f_sig")
        f_step = sem("f_step")
        f_hi = sem("f_hi")
        f_lo = sem("f_lo")
        d_used = sem("d_used")
        y_sq = sem("y_sq")
        y_step = sem("y_step")
        y_root = sem("y_root")
        y_out = sem("y_out")
        g_in = sem("g_in")
        stored = sem("stored")

        block = ctx.enter_context(nc.Block())

        def halves(use):
            return acc[use % 4][:, :, 0:HALF]

        z_tmp = [ubyb[:, KT, 0:TOK], sg[:, 0, 0:TOK]]

        def two(ap):
            return ap.rearrange("p (h t) -> p h t", h=2)

        def f(ap):
            return ap.bitcast(f32)

        @block.sync
        def _(sp):
            def load(c, slot, src, col, k0=0, kn=KT):
                if not isinstance(c, int):
                    sp.wait_ge(w_lo, c * 2 - 2)
                elif c >= 2:
                    sp.wait_ge(w_lo, 2 * c - 2)
                sp.dma_start(w_raw[:, slot, 0:kn, :], src[:, k0:k0 + kn, bass.ds(col, CW)]) \
                    .then_inc(w_loaded[slot], 16)

            for n in range(2):
                sp.dma_start(stage[n][:, :], mem_prompt[0, n * P:(n + 1) * P, :]).then_inc(row_in[n], 16)
            load(0, 0, wk, 0)
            load(1, 1, wk, CW)
            for n in range(4):
                sp.dma_start(stage[2 + n][:, :], x_prompt[0, n * P:(n + 1) * P, :]).then_inc(row_in[2 + n], 16)
            sp.dma_start(stage[6][0:TS, :], xs_dram).then_inc(row_in[6], 16)
            for n in range(2):
                sp.dma_start(stage[7 + n][0:SB_ROWS, :], sb_dram[n * SB_ROWS:(n + 1) * SB_ROWS, :]) \
                    .then_inc(row_in[7 + n], 16)
            sp.dma_start(stage[9][0:2 * TS, :], sa_dram).then_inc(row_in[9], 16)
            for c in range(2, 8):
                load(c, c % 2, wk if c < 4 else wv, (c % 4) * CW)
            sp.dma_start(conv_b_sample[0, :, 0:PAD - 1, :], state_conv_b[0, :, 1:PAD, :]).then_inc(stored, 16)
            sp.dma_start(conv_a_sample[0, :, 0:1, :], state_conv_a[0, :, 1:2, :]).then_inc(stored, 16)

            def pairs(c0, bodies, sources):
                with sp.Fori(0, bodies) as i:
                    for j in range(4):
                        src, col = sources[j % 2]
                        load(i * 4 + (c0 + j), j % 2, src, i * (2 * CW) + (col + (j // 2) * CW))

            pairs(C_B, 2, ((win, COL_BG), (win, COL_BV)))
            for j in range(4):
                load(C_Q + j, j % 2, win, COL_Q + j * CW)
            pairs(C_CX, 2, ((win, COL_AC), (win, COL_AX)))
            for j in range(8):
                load(C_X + j, j % 2, *((wox, j // 2 * CW) if j % 2 else (win, COL_GATE + BR_X * D + j // 2 * CW)))
            for j in range(4):
                load(C_BA + j, j % 2, win, COL_AB + j * CW)
            for j in range(8):
                load(C_A + j, j % 2, *((woa, j // 2 * CW) if j % 2 else (win, COL_GATE + BR_A * D + j // 2 * CW)))
            for j in range(4):
                load(C_GB + j, j % 2, win, COL_GATE + BR_B * D + j * CW)
            for j in range(4):
                load(C_OB + j, j % 2, wob, j * CW)
            for j in range(4):
                load(C_WO + j, j % 2, wo, j * CW)
            with sp.Fori(0, FT // 2) as i:
                load(i * 2 + C_F, 0, wfg, i * CW)
                load(i * 2 + (C_F + 1), 1, wfu, i * CW)
            for p in range(4):
                for g, (k0, kn) in enumerate(((0, 8), (8, 8), (16, 6))):
                    load(C_D + 3 * p + g, (3 * p + g) % 2, wfd, p * CW, k0, kn)
            sp.wait_ge(stored, 16 * 2)
            for s in range(2):
                sp.wait_ge(kv_stored[s], 16 * 4)
            sp.wait_ge(ubo_stored, 32)
            sp.wait_ge(uao_stored, 32)
            sp.wait_ge(y_out, 16 * 5)

        @block.gpsimd
        def _(pool):
            nc.gpsimd.memset(ident[:, :], 0.0).then_inc(ident_made, 1)
            nc.gpsimd.memset(ones[:, 0:4], 1.0 / D).then_inc(const_made, 1)
            nc.gpsimd.memset(ones[:, 4:8], EPS).then_inc(const_made, 1)
            nc.gpsimd.memset(st[:, :], 1.0).then_inc(stats_clear, 1)
            pool.wait_ge(ident_made, 1)
            nc.gpsimd.affine_select(out=ident[:, :], in_=ident[:, :], compare_op=ALU.not_equal, fill=1.0,
                                    base=0, pattern=[[-1, P]], channel_multiplier=1).then_inc(ident_made, 1)
            pool.wait_ge(ident_made, 2)
            nc.gpsimd.tensor_copy(ident_r[:, :], ident[0:TS, 0:TS]).then_inc(ident_made, 1)
            with pool.Fori(0, C_END // 2) as i:
                for j in range(2):
                    for s in range(2):
                        pool.wait_ge(w_hi, i * 4 + (2 * j + s + 1))
                        ks = slice(s * HK, (s + 1) * HK)
                        nc.gpsimd.tensor_tensor(w_l[:, j, ks, :], w_raw[:, j, ks, :], f(w_h[:, j, ks, :]),
                                                ALU.subtract).then_inc(w_lo, 1)

        @block.scalar
        def _(act):
            def done(use):
                act.wait_ge(acc_done, use + 1)

            def hi_part(slot):
                for s in range(2):
                    ks = slice(s * HK, (s + 1) * HK)
                    nc.scalar.activation(w_h[:, slot, ks, :], w_raw[:, slot, ks, :], ACT.Copy).then_inc(w_hi, 1)

            def split(c, slot, last_use=None):
                act.wait_ge(w_loaded[slot], (c // 2 + 1) * 16)
                if last_use is not None:
                    done(last_use)
                hi_part(slot)

            def split_in_loop(i, per_body, c0, j, last_use):
                act.wait_ge(w_loaded[j % 2], i * (8 * per_body) + 16 * ((c0 + j) // 2 + 1))
                done(last_use)
                hi_part(j % 2)

            loads = ((norm_mem, R_MEM, 1), (norm_mix, R_MIX, 1), (norm_ffn, R_FFN, 1),
                     (conv_b_bias, R_CBIAS, 1), (ln_b_g, R_LNG, 1), (ln_b_b, R_LNB, 1))
            for w, row, _n in loads:
                act.dma_start(prow[row:row + 1, :], w).then_inc(prow_in, 16)
            act.dma_start(prow[R_BG:R_BG + 3, :], b_gate[0].rearrange("(b d) -> b d", d=D)).then_inc(prow_in, 16)
            act.dma_start(prow[R_CA:R_CA + K_A, :], conv_a_w[0]).then_inc(prow_in, 16)
            act.dma_start(prow[R_CB:R_CB + K_B, :], conv_b_w[0]).then_inc(prow_in, 16)

            act.wait_ge(stats_clear, 1)

            def squares(n, rows):
                act.wait_ge(row_in[n], 16)
                if n:
                    act.wait_ge(sumsq, n)
                nc.scalar.activation(junk_norm[0:rows, :], stage[n][0:rows, :], ACT.Square,
                                     accum_out=ss[0:rows, n:n + 1]).then_inc(sumsq, 1)

            for n in range(2):
                squares(n, P)
            act.wait_ge(meansq, 1)
            nc.scalar.activation(rs_[:, 0:2], rs_[:, 0:2], ACT.Sqrt).then_inc(rootsq, 1)

            def norm_tile(n, use, dst, cols, rows):
                act.wait_ge(acc_read, use + 1)
                nc.scalar.activation(dst[:, :, cols], nrm_t[:, :, 0:rows], ACT.Copy).then_inc(nrm_hi, 1)

            norm_tile(0, T["mem"], mn[0], slice(0, P), P)
            norm_tile(1, T["mem"] + 1, mn[0], slice(P, 2 * P), P)
            split(0, 0)
            split(1, 1)
            for n in range(5):
                squares(2 + n, P if n < 4 else TS)
            act.wait_ge(meansq, 2)
            nc.scalar.activation(rs_[:, 2:7], rs_[:, 2:7], ACT.Sqrt).then_inc(rootsq, 1)

            for c in range(8):
                use = T[f"kv{c}"]
                if c >= 1:
                    split(c + 1, (c + 1) % 2, T[f"kv{c - 1}"])
                if c >= 4:
                    done(use)
                    nc.scalar.activation(vM[0][:, :, (c - 4) * CW:(c - 3) * CW], acc[use % 4][:, :, 0:CW],
                                         ACT.Copy).then_inc(kv_hi, 1)
                act.wait_ge(acc_read, use + 1)
                dst = kout if c < 4 else vout
                act.dma_start(dst[:, :, (c % 4) * CW:(c % 4 + 1) * CW], kv_f[:, c % 2, :, :]) \
                    .then_inc(kv_stored[c % 2], 16)
                if 1 <= c <= NH:
                    use = T[f"kt{c - 1}"]
                    done(use)
                    nc.scalar.activation(kT[0][:, 2 * (c - 1):2 * c, :], acc[use % 4][:, :, 0:N_MEM],
                                         ACT.Copy).then_inc(kv_hi, 1)
                if c < 5:
                    rows = P if c < 4 else TS
                    norm_tile(2 + c, T[f"prep{c}"], xn[0], slice(c * P, c * P + rows), rows)

            act.wait_ge(acc_read, T["b"])
            act.dma_start(k_st[:, :, :], kcache[:, :, 0:DH]).then_inc(k_loaded, 16)
            act.wait_ge(state_sum, 3)

            with act.Fori(0, 2) as i:
                for p in range(2):
                    u0 = i * 8 + (T["b"] + 4 * p)
                    split_in_loop(i, 4, C_B, 2 * p + 1, u0 - 1)
                    for j in range(2):
                        done(u0 + j)
                        act.wait_ge(acc_read, u0)
                        nc.scalar.activation(two(sg[:, j, 2:SG]), halves(T["b"] + 4 * p + j), ACT.Sigmoid) \
                            .then_inc(b_sig, 1)
                    split_in_loop(i, 4, C_B, 2 * p + 2, u0 + 1)

            act.wait_ge(acc_read, T["btail"] + 1)
            act.dma_start(conv_b_prompt[0, 0], ubo[0:PAD, :]).then_inc(ubo_stored, 16)
            act.dma_start(conv_b_sample[0, :, PAD - 1, :], ubo[PAD:PAD + TS, :]).then_inc(ubo_stored, 16)

            def probs_t(h):
                use = T[f"pt{h}"]
                done(use)
                nc.scalar.activation(pt_hl[0][:, :, :], acc[use % 4][:, :, :], ACT.Copy).then_inc(at_hi, 1)

            def out_t(h):
                use = T[f"o{h}"]
                done(use)
                nc.scalar.activation(br[0][:, 2 * h:2 * h + 2, 0:TP], acc[use % 4][:, :, :], ACT.Copy) \
                    .then_inc(at_hi, 1)

            for s in range(2):
                act.wait_ge(kv_stored[s], 16 * 4)
            for h in range(NH):
                split(C_Q + h + 1, (h + 1) % 2, T["b"] + 15 if h == 0 else T[f"q{h - 1}"] + 1)
                for j in range(2):
                    use = T[f"q{h}"] + j
                    done(use)
                    if h and j == 0:
                        done(T[f"s{h - 1}"])
                    nc.scalar.activation(two(q_hl[0][:, j, :]), halves(use), ACT.Copy).then_inc(q_hi, 1)
                if h:
                    probs_t(h - 1)
                    act.wait_ge(acc_read, T[f"qb{h - 1}"] + 2)
                    act.dma_start(k_st[:, :, :], kcache[:, :, h * DH:(h + 1) * DH]).then_inc(k_loaded, 16)
                    out_t(h - 1)
                use = T[f"qt{h}"]
                done(use)
                nc.scalar.activation(qs_hl[0][:, :], acc[use % 4][0:TS, 0, 0:DH], ACT.Copy).then_inc(at_hi, 1)
                use = T[f"s{h}"]
                done(use)
                if h == 0:
                    act.wait_ge(ubo_stored, 32)
                act.wait_ge(at_max, h + 1)
                for t in range(4):
                    nc.scalar.activation(p_f[:, t, :], acc[use % 4][:, t // 2, (t % 2) * N_MEM:(t % 2 + 1) * N_MEM],
                                         ACT.Exp, bias=nb[:, t:t + 1], scale=DH ** -0.5,
                                         accum_out=rsum[:, t:t + 1]).then_inc(at_exp, 1)
            probs_t(3)
            act.wait_ge(acc_read, T["qb3"] + 2)
            out_t(3)
            use = T["ss"]
            done(use)
            act.wait_ge(ss_max, 1)
            nc.scalar.activation(p32[:, :], acc[use % 4][0:NH * TS, 0, 0:N_MEM], ACT.Exp, bias=nb32,
                                 scale=DH ** -0.5, accum_out=rsum32).then_inc(ss_exp, 1)

            def load_v(i, n, head):
                act.dma_start(v_st[:, n, :, :], vcache[:, n * TS:(n + 1) * TS, bass.ds(head * DH, DH)]) \
                    .then_inc(v_loaded[n], 16)

            with act.Fori(0, 2) as i:
                head = act.snap(i * 2)
                done(i * 12 + (T["cx"] - 1))
                for n in range(2):
                    load_v(i, n, head)
                for j in range(4):
                    u0 = i * 12 + (T["cx"] + 3 * j)
                    split_in_loop(i, 4, C_CX, j + 1, u0 - 2)
                    if j % 2 == 0:
                        for n in range(2):
                            done(u0 + n)
                            if n == 0:
                                act.wait_ge(u_used, i * 4 + (j + 1))
                            nc.scalar.activation(two(sg[:, n, 2:SG]), halves(T["cx"] + 3 * j + n), ACT.Copy) \
                                .then_inc(c_copied, 1)
                    done(u0 + 2)
                    a = acc[(T["cx"] + 3 * j + 2) % 4][:, 0, 0:8].rearrange("p (e s) -> p e s", e=2)
                    h2 = i * 4 + 2 * (j // 2)
                    nc.scalar.activation(br[0][:, bass.ds(h2, 2), TP + 4 * (j % 2):TP + 4 * (j % 2) + 4], a,
                                         ACT.Copy).then_inc(v_hi, 1)
                    if j < 2:
                        load_v(i, j, head + 1)

            act.wait_ge(acc_read, T["ctail"] + 1)
            act.dma_start(conv_a_prompt[0, 0], uao[0:2, :]).then_inc(uao_stored, 16)
            act.dma_start(conv_a_sample[0, :, 1, :], uao[2:2 + TS, :]).then_inc(uao_stored, 16)

            def gate_stage(t0, c0, row, sig):
                with act.Fori(0, 2) as i:
                    for p in range(2):
                        u0 = i * 8 + (t0 + 4 * p)
                        split_in_loop(i, 4, c0, 2 * p + 1, u0 - 1)
                        for j in range(2):
                            done(u0 + j)
                            act.wait_ge(acc_read, u0)
                            nc.scalar.activation(two(sg[:, j, 2:SG]), halves(t0 + 4 * p + j), ACT.Sigmoid,
                                                 bias=param(i * 4 + (2 * p + j), row)).then_inc(sig, 1)
                        split_in_loop(i, 4, c0, 2 * p + 2, u0 + 1)

            act.wait_ge(u_used, 1 + KT)
            gate_stage(T["x"], C_X, R_BG + BR_X, x_sig)

            for n in range(KT):
                if n % 2 == 0:
                    split(C_BA + n // 2 + 1, (n // 2 + 1) % 2, T["ba"] + n - 1)
                act.wait_ge(acc_read, T["ba"] + n + 1)
                nc.scalar.activation(br[0][:, n, :], yA[:, n, :], ACT.Copy).then_inc(ba_hi, 1)

            gate_stage(T["a"], C_A, R_BG + BR_A, a_sig)

            def gate_b(n, use):
                if n % 2 == 0:
                    split(C_GB + n // 2 + 1, (n // 2 + 1) % 2, use - 1)
                done(use)
                if n == 0:
                    act.wait_ge(ba_lo, KT)
                nc.scalar.activation(two(sgB[:, n, :]), halves(use), ACT.Sigmoid,
                                     bias=prm[:, n, R_BG + BR_B:R_BG + BR_B + 1]).then_inc(gb_sig, 1)

            def ln_square(k):
                act.wait_ge(ln_sub, k + 1)
                if k >= 2:
                    act.wait_ge(ln_acc, k - 1)
                nc.scalar.activation(sg[:, k % 2, 0:TOK], ubyb[:, k, 0:TOK], ACT.Square).then_inc(ln_sq, 1)

            gb = T["gb"]
            gate_b(0, gb)
            gate_b(1, gb + 1)
            for k in range(4):
                ln_square(k)
            gate_b(2, gb + 3)
            gate_b(3, gb + 4)
            for k in range(4, 8):
                ln_square(k)
            gate_b(4, gb + 5)
            gate_b(5, gb + 6)
            done(gb + 7)
            nc.scalar.activation(two(sg[:, 1, 0:TOK]), halves(gb + 7), ACT.Sqrt, bias=eps).then_inc(ln_root, 1)
            gate_b(6, gb + 8)
            gate_b(7, gb + 9)
            for k in range(KT + 1):
                if k < KT:
                    act.wait_ge(z_aff, k + 1)
                    if k >= 2:
                        act.wait_ge(z_f, k - 1)
                    nc.scalar.activation(z_tmp[k % 2], ubyb[:, k, 0:TOK], ACT.Sigmoid, bias=param(k, R_LNB)) \
                        .then_inc(z_sig, 1)
                if k:
                    act.wait_ge(z_f, k)
                    nc.scalar.activation(zb[0][:, k - 1, :], ubyb[:, k - 1, 0:TOK], ACT.Copy).then_inc(z_hi, 1)

            for n in range(KT):
                if n % 2 == 0:
                    split(C_OB + n // 2 + 1, (n // 2 + 1) % 2, T["ob"] + n - 1)
                act.wait_ge(m_sum, n + 1)
                nc.scalar.activation(br[0][:, n, :], merged[:, n, :], ACT.Copy).then_inc(m_hi, 1)

            done(T["ob"] + 7)
            for t in range(4):
                act.dma_start(x_st[:, t, :], x_prompt[0, t * P:(t + 1) * P, :]).then_inc(x_again, 16)
            act.dma_start(xs_st[:, :], xs_dram).then_inc(x_again, 16)

            for n in range(KT):
                if n % 2 == 0:
                    split(C_WO + n // 2 + 1, (n // 2 + 1) % 2, T["wo"] + n - 1)
                use = T["wo"] + n
                done(use)
                if n >= 2:
                    act.wait_ge(h_sum, n - 1)
                nc.scalar.activation(two(sg[:, n % 2, 0:TOK]), halves(use), ACT.Square).then_inc(h_sq, 1)
                if n == 0:
                    act.wait_ge(m_lo, KT)
                nc.scalar.activation(two(hg[0][:, n, :]), halves(use), ACT.Copy,
                                     scale=prm[:, n, R_FFN:R_FFN + 1]).then_inc(h_hi, 1)
            done(T["r"])
            nc.scalar.activation(two(sg[:, 0, 0:TOK]), halves(T["r"]), ACT.Sqrt, bias=eps).then_inc(r_root, 1)

            with act.Fori(0, FT // 2) as i:
                u0 = i * 4 + T["f"]
                split_in_loop(i, 2, C_F, 1, u0 - 1)
                for j in range(2):
                    act.wait_ge(acc_read, u0 + (j + 1))
                    nc.scalar.activation(sgf[:, j, :], sg[:, j, 0:TOK], ACT.Sigmoid).then_inc(f_sig, 1)
                split_in_loop(i, 2, C_F, 2, u0 + 1)
                for j in range(2):
                    act.wait_ge(acc_read, u0 + (3 + j))
                    nc.scalar.activation(mid_f[0][:, bass.ds(i * (2 * TOK) + j * TOK, TOK)], sg[:, j, 0:TOK],
                                         ACT.Copy).then_inc(f_hi, 1)

            act.wait_ge(acc_read, T["d0"])
            act.dma_start(gfin[:, :], norm_final.rearrange("(a d) -> a d", a=1).broadcast_to([P, D])) \
                .then_inc(g_in, 16)
            for c in range(C_D + 1, C_END):
                p, g = divmod(c - 2 - C_D, 3)
                if c == C_D + 1:
                    done(T["f"] + 2 * FT - 1)
                elif g == 2:
                    done(T[f"d{p}"] + 1)
                else:
                    act.wait_ge(d_used, 2 * p + g + 1)
                act.wait_ge(w_loaded[c % 2], (c // 2 + 1) * 16)
                hi_part(c % 2)
            y_cols = ((0, 6 * P, T["y2"] + 2), (6 * P, D, T["y3"] + 2))
            n = 0
            for part_n, (a, b, read) in enumerate(y_cols):
                act.wait_ge(acc_read, read)
                for t in range(5):
                    src = y_st[:, t, a:b] if t < 4 else ys_st[:, a:b]
                    rows = P if t < 4 else TS
                    if n:
                        act.wait_ge(y_sq, n)
                    nc.scalar.activation(junk[0:rows, 0:b - a], src, ACT.Square,
                                         accum_out=ssy[0:rows, 5 * part_n + t:5 * part_n + t + 1]).then_inc(y_sq, 1)
                    n += 1
            act.wait_ge(y_step, 2)
            nc.scalar.activation(rfin[:, :], rfin[:, :], ACT.Sqrt).then_inc(y_root, 1)
            for t in range(5):
                act.wait_ge(y_step, 4 + t)
                if t < 4:
                    act.dma_start(y_prompt[0, t * P:(t + 1) * P, :], y_st[:, t, :]).then_inc(y_out, 16)
                else:
                    act.dma_start(y_sample.rearrange("s t d -> (s t) d"), ys_st[:, :]).then_inc(y_out, 16)

        @block.vector
        def _(dve):
            V = nc.vector

            def done(use):
                dve.wait_ge(acc_done, use + 1)

            dve.wait_ge(stats_clear, 1)

            def norm_rows(batch, a, b):
                dve.wait_ge(sumsq, b)
                V.tensor_scalar(rs_[:, a:b], ss[:, a:b], 1.0 / D, EPS, ALU.mult, ALU.add).then_inc(meansq, 1)
                dve.wait_ge(rootsq, batch + 1)
                V.reciprocal(rs_[:, a:b], rs_[:, a:b]).then_inc(pads, 1)
                dve.wait_ge(pads, batch + 1)
                for n in range(a, b):
                    rows = TS if n == 6 else P
                    V.tensor_scalar(stage[n][0:rows, :], stage[n][0:rows, :], rs_[0:rows, n:n + 1], None,
                                    ALU.mult).then_inc(row_scaled, 1)

            def blocks(use, rows):
                return acc[use % 4][:, :, :].rearrange("p b (k r) -> p (b k) r", r=P)[:, :, 0:rows]

            norm_rows(0, 0, 2)
            done(T["param"])
            V.tensor_copy(prm[:, :, :], blocks(T["param"], R_ALL)).then_inc(acc_read, 1)
            dve.wait_ge(acc_read, 1)
            lo_count = 0

            def norm_tile(use, gain_row, dst, cols, rows):
                nonlocal lo_count
                done(use)
                if lo_count:
                    dve.wait_ge(nrm_lo, lo_count)
                V.tensor_tensor(nrm_t[:, :, 0:rows], blocks(use, rows),
                                prm[:, :, gain_row:gain_row + 1].broadcast_to([P, KT, rows]),
                                ALU.mult).then_inc(acc_read, 1)
                lo_count += 1
                dve.wait_ge(nrm_hi, lo_count)
                V.tensor_tensor(dst[1][:, :, cols], nrm_t[:, :, 0:rows], f(dst[0][:, :, cols]),
                                ALU.subtract).then_inc(nrm_lo, 1)

            norm_tile(T["mem"], R_MEM, mn, slice(0, P), P)
            norm_tile(T["mem"] + 1, R_MEM, mn, slice(P, 2 * P), P)
            norm_rows(1, 2, 7)

            hi_count = 0
            for c in range(8):
                use = T[f"kv{c}"]
                done(use)
                if c >= 4:
                    hi_count += 1
                    dve.wait_ge(kv_hi, hi_count)
                    cols = slice((c - 4) * CW, (c - 3) * CW)
                    V.tensor_tensor(vM[1][:, :, cols], acc[use % 4][:, :, 0:CW], f(vM[0][:, :, cols]),
                                    ALU.subtract).then_inc(kv_lo, 1)
                if c >= 2:
                    dve.wait_ge(kv_stored[c % 2], 16 * (c // 2))
                V.tensor_copy(kv_f[:, c % 2, :, :], acc[use % 4][:, :, 0:CW]).then_inc(acc_read, 1)
                if 1 <= c <= NH:
                    use = T[f"kt{c - 1}"]
                    done(use)
                    hi_count += 1
                    dve.wait_ge(kv_hi, hi_count)
                    V.tensor_tensor(kT[1][:, 2 * c - 2:2 * c, :], acc[use % 4][:, :, 0:N_MEM],
                                    f(kT[0][:, 2 * c - 2:2 * c, :]), ALU.subtract).then_inc(acc_read, 1)
                use = T[f"prep{c}"]
                if c < 5:
                    rows = P if c < 4 else TS
                    norm_tile(use, R_MIX, xn, slice(c * P, c * P + rows), rows)
                    continue
                done(use)
                taps, row, samples = (PAD, R_CB, TS // 2) if c < 7 else (K_A - 1, R_CA, TS)
                prod = nrm_t[:, :, 0:samples * taps].rearrange("p k (s j) -> p k s j", j=taps)
                w = prm[:, :, row:row + taps].rearrange("p k (s j) -> p k s j", s=1) \
                    .broadcast_to([P, KT, samples, taps])
                if c > 5:
                    dve.wait_ge(state_sum, c - 5)
                else:
                    dve.wait_ge(nrm_lo, lo_count)
                V.tensor_tensor(prod, blocks(use, samples * taps).rearrange("p k (s j) -> p k s j", j=taps), w,
                                ALU.mult).then_inc(acc_read, 1)
                dve.wait_ge(acc_read, use + 1)
                dst = ysb[:, :, (c - 5) * samples:(c - 4) * samples] if c < 7 else ysa[:, :, :]
                V.tensor_reduce(dst, prod, AX.X, ALU.add).then_inc(state_sum, 1)
            dve.wait_ge(state_sum, 3)
            V.tensor_tensor(ysb[:, :, :], ysb[:, :, :],
                            prm[:, :, R_CBIAS:R_CBIAS + 1].broadcast_to([P, KT, TS]), ALU.add).then_inc(state_sum, 1)
            V.memset(ubyb[:, 1:KT + 1, 0:PAD], 0.0).then_inc(pads, 1)

            with dve.Fori(0, 2) as i:
                for p in range(2):
                    u0 = i * 8 + (T["b"] + 4 * p)
                    dve.wait_ge(b_sig, i * 4 + (2 * p + 2))
                    for j in range(2):
                        done(u0 + (2 + j))
                        dst = ubyb_f[:, bass.ds(i * (4 * SLOT) + ((2 * p + j + 1) * SLOT + PAD), TOK)]
                        V.tensor_tensor(two(dst), halves(T["b"] + 4 * p + 2 + j), two(sg[:, j, 2:SG]),
                                        ALU.mult).then_inc(acc_read, 1 if j else 3)

            done(T["btail"])
            V.tensor_copy(ubo[:, :].rearrange("p (b c) -> p b c", b=2),
                          acc[T["btail"] % 4][0:PAD + TS, :, :]).then_inc(acc_read, 1)

            CV = K_B + 1

            def conv(tile, steps):
                y = ubyb_f[:, bass.ds(tile * SLOT, TP)]
                for k in steps:
                    if k == 0:
                        if not isinstance(tile, int) or tile:
                            dve.wait_ge(cv_step, tile * CV)
                        ins = V.scalar_tensor_tensor(
                            ubyb_f[:, bass.ds(tile * SLOT + TP, TS)], ubyb_f[:, bass.ds(tile * SLOT + (SLOT + PAD + TP), TS)],
                            param(tile, R_CB + K_B - 1), flat(ysb)[:, bass.ds(tile * TS, TS)], ALU.mult, ALU.add)
                    else:
                        u = ubyb_f[:, bass.ds(tile * SLOT + (SLOT + k - 1), TP)]
                        w = param(tile, R_CB + k - 1)
                        if k == 1:
                            ins = V.tensor_scalar(y, u, w, param(tile, R_CBIAS), ALU.mult, ALU.add)
                        else:
                            dve.wait_ge(cv_step, tile * CV + k)
                            ins = V.scalar_tensor_tensor(y, u, w, y, ALU.mult, ALU.add)
                    ins.then_inc(cv_step, 1)

            Q4 = (range(0, 12), range(12, 16), range(16, 28), range(28, 32))
            R4 = (range(0, 8), range(8, 16), range(16, 24), range(24, 32))

            dve.wait_ge(acc_read, T["btail"] + 1)
            dve.wait_ge(pads, 3)
            hi_count = 0

            def lo_part(use, dst, src):
                nonlocal hi_count
                hi_count += 1
                done(use)
                dve.wait_ge(at_hi, hi_count)
                V.tensor_tensor(dst[1], src, f(dst[0]), ALU.subtract).then_inc(acc_read, 1)

            def head_tail(h):
                use = T[f"pt{h}"]
                lo_part(use, [q[:, :, :] for q in pt_hl], acc[use % 4][:, :, :])
                dve.wait_ge(k_loaded, 16 * (h + 1))
                for u in range(2):
                    use = T[f"qb{h}"] + u
                    done(use)
                    for s in range(4):
                        for m in range(2):
                            a = (4 * u + s) * 2 + m
                            col = (4 * u + s) * NH + h
                            ins = V.scalar_tensor_tensor(
                                k_st[:, a, :], k_st[:, a, :], 1.0, acc[use % 4][:, s // 2, (s % 2) * DH:(s % 2 + 1) * DH],
                                ALU.mult, ALU.mult, accum_out=sc[:, m, col:col + 1])
                    ins.then_inc(acc_read, 1)
                use = T[f"o{h}"]
                lo_part(use, [b[:, 2 * h:2 * h + 2, 0:TP] for b in br], acc[use % 4][:, :, :])

            for h in range(NH):
                for j in range(2):
                    use = T[f"q{h}"] + j
                    done(use)
                    dve.wait_ge(q_hi, 2 * h + j + 1)
                    V.tensor_copy(qs_f[:, j, :], acc[use % 4][:, 1, HALF - TS:HALF])
                    V.tensor_tensor(two(q_hl[1][:, j, :]), halves(use), two(f(q_hl[0][:, j, :])),
                                    ALU.subtract).then_inc(acc_read, 1)
                if h:
                    head_tail(h - 1)
                use = T[f"qt{h}"]
                lo_part(use, [q[:, :] for q in qs_hl], acc[use % 4][0:TS, 0, 0:DH])
                use = T[f"s{h}"]
                done(use)
                scores = acc[use % 4][:, :, :].rearrange("p b (t m) -> p (b t) m", m=N_MEM)
                V.reduce_max(mx[:, :], scores, AX.X).then_inc(at_step, 1)
                dve.wait_ge(at_step, 3 * h + 1)
                V.tensor_scalar(nb[:, :], mx[:, :], -(DH ** -0.5), None, ALU.mult).then_inc(at_max, 1)
                conv(0, R4[h][:4])
                dve.wait_ge(at_exp, 4 * h + 4)
                V.reciprocal(rrec[:, :], rsum[:, :]).then_inc(at_step, 1)
                dve.wait_ge(at_step, 3 * h + 2)
                V.tensor_tensor(p_f[:, :, :], p_f[:, :, :],
                                rrec[:, :].rearrange("p (t m) -> p t m", m=1).broadcast_to([P, 4, N_MEM]),
                                ALU.mult).then_inc(acc_read, 1)
                V.memset(mx[:, 0:1], 0.0).then_inc(at_step, 1)
                conv(0, R4[h][4:])
            head_tail(3)
            use = T["ss"]
            done(use)
            V.reduce_max(mx32, acc[use % 4][0:NH * TS, 0, 0:N_MEM], AX.X).then_inc(ss_step, 1)
            dve.wait_ge(ss_step, 1)
            V.tensor_scalar(nb32, mx32, -(DH ** -0.5), None, ALU.mult).then_inc(ss_max, 1)
            dve.wait_ge(ss_exp, 1)
            V.reciprocal(rrec32, rsum32).then_inc(ss_step, 1)
            dve.wait_ge(ss_step, 2)
            V.tensor_scalar(p32[:, :], p32[:, :], rrec32, None, ALU.mult).then_inc(acc_read, 1)
            use = T["sp"]
            done(use)
            V.tensor_copy(pT[:, :, :], acc[use % 4][:, 0, 0:2 * NH * TS].rearrange("p (m c) -> p m c", m=2)) \
                .then_inc(acc_read, 1)
            V.memset(sg[:, :, 0:2], 0.0).then_inc(u_used, 1)

            with dve.Fori(0, 2) as i:
                for p in range(2):
                    u0 = i * 12 + (T["cx"] + 6 * p)

                    def piece(n, use, static, release):
                        done(use)
                        dve.wait_ge(v_hi, i * 4 + (2 * p + n + 1))
                        cols = slice(TP + 4 * n, TP + 4 * n + 4)
                        h2 = bass.ds(i * 4 + 2 * p, 2)
                        V.tensor_tensor(br[1][:, h2, cols], acc[static % 4][:, 0, 0:8].rearrange("p (e s) -> p e s", e=2),
                                        f(br[0][:, h2, cols]), ALU.subtract).then_inc(acc_read, release)

                    dve.wait_ge(c_copied, i * 4 + (2 * p + 2))
                    piece(0, u0 + 2, T["cx"] + 6 * p + 2, 3)
                    conv(i + 1, Q4[2 * p][:6])
                    for j in range(2):
                        n = i * 4 + (2 * p + j)
                        done(u0 + (3 + j))
                        V.tensor_tensor(two(sg[:, j, 2:SG]), halves(T["cx"] + 6 * p + 3 + j), two(sg[:, j, 2:SG]),
                                        ALU.mult).then_inc(acc_read, 1)
                        dve.wait_ge(acc_read, u0 + (4 + j))
                        if j:
                            piece(1, u0 + 5, T["cx"] + 6 * p + 5, 1)
                        y = yA_f[:, bass.ds(n * TOK, TP)]
                        V.tensor_scalar(y, sg[:, j, 0:TP], param(n, R_CA), None, ALU.mult).then_inc(ca_step, 1)
                        V.scalar_tensor_tensor(yA_f[:, bass.ds(n * TOK + TP, TS)], sg[:, j, SG - TS:SG],
                                               param(n, R_CA + 2), flat(ysa)[:, bass.ds(n * TS, TS)], ALU.mult, ALU.add)
                        V.tensor_copy(flat(ua_tail)[:, bass.ds(n * (TS + 2), TS + 2)], sg[:, j, SG - TS - 2:SG])
                        for k in (1, 2):
                            dve.wait_ge(ca_step, i * 8 + (4 * p + 2 * j + k))
                            V.scalar_tensor_tensor(y, sg[:, j, k:k + TP], param(n, R_CA + k), y, ALU.mult, ALU.add) \
                                .then_inc(ca_step if k == 1 else u_used, 1)
                        conv(i + 1, Q4[2 * p][6:] if j == 0 else Q4[2 * p + 1])

            done(T["ctail"])
            V.tensor_copy(uao[:, :].rearrange("p (b c) -> p b c", b=2), acc[T["ctail"] % 4][0:TS + 2, :, :]) \
                .then_inc(acc_read, 1)

            dve.wait_ge(uao_stored, 32)
            with dve.Fori(0, 2) as i:
                for p in range(2):
                    u0 = i * 8 + (T["x"] + 4 * p)
                    conv(i + 3, Q4[2 * p])
                    dve.wait_ge(x_sig, i * 4 + (2 * p + 2))
                    for j in range(2):
                        done(u0 + (2 + j))
                        dst = merged_f[:, bass.ds(i * (4 * TOK) + (2 * p + j) * TOK, TOK)]
                        V.tensor_tensor(two(dst), halves(T["x"] + 4 * p + 2 + j), two(sg[:, j, 2:SG]),
                                        ALU.mult).then_inc(acc_read, 1 if j else 3)
                        if j == 0:
                            conv(i + 3, Q4[2 * p + 1])

            def ba_lo_part(n):
                dve.wait_ge(ba_hi, n + 1)
                V.tensor_tensor(br[1][:, n, :], yA[:, n, :], f(br[0][:, n, :]), ALU.subtract).then_inc(ba_lo, 1)

            dve.wait_ge(u_used, 1 + KT)
            for n in range(KT):
                done(T["ba"] + n)
                V.tensor_tensor(two(yA[:, n, :]), halves(T["ba"] + n), two(yA[:, n, :]), ALU.mult) \
                    .then_inc(acc_read, 1)
                if n:
                    ba_lo_part(n - 1)
                conv(5, range(4 * n, 4 * n + 4))
            ba_lo_part(KT - 1)

            with dve.Fori(0, 2) as i:
                for p in range(2):
                    u0 = i * 8 + (T["a"] + 4 * p)
                    conv(i + 6, Q4[2 * p])
                    dve.wait_ge(a_sig, i * 4 + (2 * p + 2))
                    for j in range(2):
                        done(u0 + (2 + j))
                        V.tensor_tensor(two(sg[:, j, 2:SG]), halves(T["a"] + 4 * p + 2 + j), two(sg[:, j, 2:SG]),
                                        ALU.mult).then_inc(a_step, 1)
                        dve.wait_ge(a_step, i * 4 + (2 * p + j + 1))
                        dst = merged_f[:, bass.ds(i * (4 * TOK) + (2 * p + j) * TOK, TOK)]
                        V.tensor_tensor(dst, dst, sg[:, j, 2:SG], ALU.add).then_inc(acc_read, 1 if j else 3)
                        if j == 0:
                            conv(i + 6, Q4[2 * p + 1])

            gb = T["gb"]
            dve.wait_ge(cv_step, KT * CV)
            total = ubyb[:, KT, 0:TOK]
            for k in range(1, KT):
                V.tensor_tensor(total, ubyb[:, k, 0:TOK], ubyb[:, 0, 0:TOK] if k == 1 else total, ALU.add) \
                    .then_inc(ln_step, 1)
                dve.wait_ge(ln_step, k)
            done(gb + 2)
            dve.wait_ge(gb_sig, 2)
            for k in range(KT):
                ins = V.tensor_tensor(two(ubyb[:, k, 0:TOK]), two(ubyb[:, k, 0:TOK]), halves(gb + 2), ALU.subtract)
                ins.then_inc(ln_sub, 1)
            dve.wait_ge(ln_sq, 1)
            V.tensor_copy(total, sg[:, 0, 0:TOK]).then_inc(acc_read, 3)
            dve.wait_ge(acc_read, gb + 3)
            for k in range(1, KT):
                dve.wait_ge(ln_sq, k + 1)
                V.tensor_tensor(total, total, sg[:, k % 2, 0:TOK], ALU.add).then_inc(ln_acc, 1)
                dve.wait_ge(ln_acc, k)
                if k in (5, 7):
                    dve.wait_ge(gb_sig, k - 1)
                    V.memset(mx[:, 0:1], 0.0).then_inc(acc_read, 2)
            done(gb + 7)
            dve.wait_ge(ln_root, 1)
            V.reciprocal(sg[:, 1, 0:TOK], sg[:, 1, 0:TOK]).then_inc(acc_read, 1)
            dve.wait_ge(acc_read, gb + 8)

            def affine(k):
                V.scalar_tensor_tensor(ubyb[:, k, 0:TOK], ubyb[:, k, 0:TOK], param(k, R_LNG), sg[:, 1, 0:TOK],
                                       ALU.mult, ALU.mult).then_inc(z_aff, 1)

            def z_lo_part(k):
                dve.wait_ge(z_hi, k + 1)
                V.tensor_tensor(zb[1][:, k, :], ubyb[:, k, 0:TOK], f(zb[0][:, k, :]), ALU.subtract) \
                    .then_inc(z_lo, 1)

            dve.wait_ge(ln_sub, KT)
            affine(0)
            for k in range(KT):
                if k + 1 < KT:
                    affine(k + 1)
                dve.wait_ge(z_sig, k + 1)
                V.scalar_tensor_tensor(ubyb[:, k, 0:TOK], ubyb[:, k, 0:TOK], param(k, R_LNB), z_tmp[k % 2],
                                       ALU.add, ALU.mult).then_inc(z_f, 1)
                if k:
                    z_lo_part(k - 1)
            z_lo_part(KT - 1)

            def m_lo_part(n):
                dve.wait_ge(m_hi, n + 1)
                V.tensor_tensor(br[1][:, n, :], merged[:, n, :], f(br[0][:, n, :]), ALU.subtract).then_inc(m_lo, 1)

            dve.wait_ge(gb_sig, KT)
            for n in range(KT):
                done(T["ob"] + n)
                V.tensor_tensor(two(sgB[:, n, :]), halves(T["ob"] + n), two(sgB[:, n, :]), ALU.mult) \
                    .then_inc(acc_read, 1 if n else 3)
                dve.wait_ge(acc_read, T["ob"] + n + 1)
                V.tensor_tensor(merged[:, n, :], merged[:, n, :], sgB[:, n, :], ALU.add).then_inc(m_sum, 1)
                if n:
                    m_lo_part(n - 1)
            m_lo_part(KT - 1)

            for n in range(KT):
                use = T["wo"] + n
                done(use)
                dve.wait_ge(h_hi, n + 1)
                V.tensor_copy(two(h_sb[:, n, :]), halves(use))
                if n == 0:
                    V.tensor_copy(hsum[:, :], sg[:, 0, 0:TOK]).then_inc(h_sum, 1)
                else:
                    dve.wait_ge(h_sum, n)
                    V.tensor_tensor(hsum[:, :], hsum[:, :], sg[:, n % 2, 0:TOK], ALU.add).then_inc(h_sum, 1)
                V.scalar_tensor_tensor(two(hg[1][:, n, :]), halves(use), param(n, R_FFN), two(f(hg[0][:, n, :])),
                                       ALU.mult, ALU.subtract).then_inc(acc_read, 1)
            done(T["r"])
            dve.wait_ge(r_root, 1)
            V.reciprocal(rms[:, :], sg[:, 0, 0:TOK]).then_inc(acc_read, 1)
            dve.wait_ge(acc_read, T["r"] + 1)

            V.memset(mx[:, 0:1], 0.0).then_inc(f_lo, 2)
            with dve.Fori(0, FT // 2) as i:
                u0 = i * 4 + T["f"]
                for j in range(2):
                    done(u0 + j)
                    dve.wait_ge(f_lo, i * 2 + (j + 1))
                    V.tensor_tensor(two(sg[:, j, 0:TOK]), halves(T["f"] + j), two(rms[:, :]), ALU.mult) \
                        .then_inc(acc_read, 1)
                for j in range(2):
                    dve.wait_ge(f_sig, i * 2 + (j + 1))
                    V.tensor_tensor(sg[:, j, 0:TOK], sg[:, j, 0:TOK], sgf[:, j, :], ALU.mult).then_inc(f_step, 1)
                for j in range(2):
                    dve.wait_ge(f_step, i * 4 + (j + 1))
                    V.tensor_tensor(sg[:, j, 0:TOK], sg[:, j, 0:TOK], rms[:, :], ALU.mult).then_inc(f_step, 1)
                for j in range(2):
                    done(u0 + (2 + j))
                    dve.wait_ge(f_step, i * 4 + (j + 3))
                    V.tensor_tensor(two(sg[:, j, 0:TOK]), halves(T["f"] + 2 + j), two(sg[:, j, 0:TOK]), ALU.mult) \
                        .then_inc(acc_read, 1)
                for j in range(2):
                    dve.wait_ge(f_hi, i * 2 + (j + 1))
                    cols = bass.ds(i * (2 * TOK) + j * TOK, TOK)
                    V.tensor_tensor(mid_f[1][:, cols], sg[:, j, 0:TOK], f(mid_f[0][:, cols]), ALU.subtract) \
                        .then_inc(f_lo, 1)

            def rows_out(p):
                for j in range(2):
                    use = T[f"y{p}"] + j
                    cols = slice((2 * p + j) * P, (2 * p + j + 1) * P)
                    done(use)
                    V.tensor_copy(y_st[:, :, cols], acc[use % 4][:, 0, :].rearrange("p (t c) -> p t c", c=P))
                    V.tensor_copy(ys_st[:, cols], acc[use % 4][0:TS, 1, 0:P]).then_inc(acc_read, 1)

            for p in range(4):
                for j in range(2):
                    n, use = 2 * p + j, T[f"d{p}"] + j
                    done(use)
                    V.tensor_tensor(two(h_sb[:, n, :]), halves(use), two(h_sb[:, n, :]), ALU.add) \
                        .then_inc(acc_read, 1)
                if p:
                    rows_out(p - 1)
            rows_out(3)
            dve.wait_ge(y_sq, 10)
            V.tensor_tensor(rfin[:, :], ssy[:, 0:5], ssy[:, 5:10], ALU.add).then_inc(y_step, 1)
            dve.wait_ge(y_step, 1)
            V.tensor_scalar(rfin[:, :], rfin[:, :], 1.0 / D, EPS, ALU.mult, ALU.add).then_inc(y_step, 1)
            dve.wait_ge(y_root, 1)
            V.reciprocal(rfin[:, :], rfin[:, :]).then_inc(y_step, 1)
            dve.wait_ge(y_step, 3)
            dve.wait_ge(g_in, 16)
            for t in range(5):
                rows = P if t < 4 else TS
                y = y_st[:, t, :] if t < 4 else ys_st[:, :]
                V.scalar_tensor_tensor(y, y, rfin[0:rows, t:t + 1], gfin[0:rows, :], ALU.mult, ALU.mult) \
                    .then_inc(y_step, 1)

        @block.tensor
        def _(pe):
            M = nc.tensor

            def free(use):
                if not isinstance(use, int) or use >= 4:
                    pe.wait_ge(acc_read, use - 3)

            def flip(out, src, ident_ap=None, last=False):
                rows = src.shape[0]
                return M.transpose(out, src, ident[0:rows, 0:rows])

            def flip8(use, src, rows, width=P):
                for k in range(KT):
                    last = flip(acc[use % 4][:, k // 4, (k % 4) * P:(k % 4) * P + rows], src[0:rows, k * P:(k + 1) * P])
                last.then_inc(acc_done, 1)

            def flip8_back(use, src, cols, count):
                for k in range(KT):
                    last = flip(acc[use % 4][0:count, k // 4, (k % 4) * P:(k % 4 + 1) * P], src(k)[:, cols])
                last.then_inc(acc_done, 1)

            def weights(half):
                pe.wait_ge(w_lo, half)

            def tile(slot, j, use, x, k_at=0, ks=KT, start=True, stop=True, first_half=None):
                out = acc[use % 4]
                for k in range(ks):
                    if first_half is not None and k % HK == 0:
                        weights(first_half(k // HK))
                    cols = slice(j * P, (j + 1) * P)
                    wh, wl = w_h[:, slot, k, cols], w_l[:, slot, k, cols]
                    for w, xs in ((wh, x[0]), (wh, x[1]), (wl, x[0])):
                        for b in range(2):
                            last = M.matmul(out[:, b, 0:HALF], w, xs[:, k_at + k, b * HALF:(b + 1) * HALF],
                                            start=start and k == 0 and w is wh and xs is x[0],
                                            stop=stop and k == ks - 1 and w is wl)
                return last

            def chunk(c, slot, use, static, x, ready=None):
                for j in range(2):
                    free(use + j)
                    tile(slot, j, static + j, x,
                         first_half=None if j else (lambda s: c * 2 + (s + 1))).then_inc(acc_done, 1)

            pe.wait_ge(ident_made, 3)
            pe.wait_ge(prow_in, 16 * 9)
            flip8(T["param"], prow, R_ALL)
            for n in range(2):
                pe.wait_ge(row_scaled, n + 1)
                flip8(T["mem"] + n, stage[n], P)

            pe.wait_ge(nrm_lo, 2)
            for c in range(8):
                use = T[f"kv{c}"]
                free(use)
                for m in range(2):
                    for k in range(KT):
                        if m == 0 and k % HK == 0:
                            weights(2 * c + k // HK + 1)
                        rows = slice(m * P, (m + 1) * P)
                        for n, (x, w) in enumerate(((mn[0], w_h), (mn[0], w_l), (mn[1], w_h))):
                            last = M.matmul(acc[use % 4][:, m, 0:CW], x[:, k, rows], w[:, c % 2, k, :],
                                            start=k == 0 and n == 0, stop=k == KT - 1 and n == 2)
                last.then_inc(acc_done, 1)
                if 1 <= c <= NH:
                    use = T[f"kt{c - 1}"]
                    free(use)
                    pe.wait_ge(acc_read, T[f"kv{c - 1}"] + 1)
                    for e in range(2):
                        for m in range(2):
                            last = flip(acc[use % 4][:, e, m * P:(m + 1) * P],
                                        kv_f[:, (c - 1) % 2, m, e * P:(e + 1) * P])
                    last.then_inc(acc_done, 1)
                use = T[f"prep{c}"]
                free(use)
                if c < 5:
                    pe.wait_ge(row_scaled, c + 3)
                else:
                    pe.wait_ge(row_in[c + 2], 16)
                flip8(use, stage[c + 2], (P, P, P, P, TS, SB_ROWS, SB_ROWS, 2 * TS)[c])

            pe.wait_ge(nrm_lo, 7)
            pe.wait_ge(kv_lo, 4)

            def pairs(t0, c0, xs):
                with pe.Fori(0, 2) as i:
                    for j in range(4):
                        chunk(i * 4 + (c0 + j), j % 2, i * 8 + (t0 + 2 * j), t0 + 2 * j, xs[j % 2])

            pairs(T["b"], C_B, (xn, xn))
            use = T["btail"]
            free(use)
            pe.wait_ge(acc_read, use)
            flip8_back(use, lambda k: ubyb[:, k + 1, :], slice(SLOT - TS - PAD, SLOT), PAD + TS)

            def head_tail(h):
                use = T[f"pt{h}"]
                free(use)
                pe.wait_ge(acc_read, T[f"s{h}"] + 1)
                for t in range(4):
                    for m in range(2):
                        last = flip(acc[use % 4][:, m, t * P:(t + 1) * P], p_f[:, t, m * P:(m + 1) * P])
                last.then_inc(acc_done, 1)
                pe.wait_ge(acc_read, T[f"qt{h}"] + 1)
                for u in range(2):
                    use = T[f"qb{h}"] + u
                    free(use)
                    for s in range(4):
                        row = ident_r[:, 4 * u + s:4 * u + s + 1].broadcast_to([TS, P])
                        for n in range(2):
                            last = M.matmul(acc[use % 4][:, s // 2, (s % 2) * DH:(s % 2 + 1) * DH], row,
                                            qs_hl[n][:, :], start=n == 0, stop=n == 1)
                    last.then_inc(acc_done, 1)
                use = T[f"o{h}"]
                free(use)
                pe.wait_ge(acc_read, T[f"pt{h}"] + 1)
                for e in range(2):
                    for m in range(2):
                        cols = slice(h * DH + e * P, h * DH + (e + 1) * P)
                        for n, (v, p) in enumerate(((0, 0), (0, 1), (1, 0))):
                            last = M.matmul(acc[use % 4][:, e, :], vM[v][:, m, cols], pt_hl[p][:, m, :],
                                            start=m == 0 and n == 0, stop=m == 1 and n == 2)
                last.then_inc(acc_done, 1)

            for h in range(NH):
                chunk(C_Q + h, h % 2, T[f"q{h}"], T[f"q{h}"], xn)
                if h:
                    head_tail(h - 1)
                use = T[f"qt{h}"]
                free(use)
                pe.wait_ge(acc_read, T[f"q{h}"] + 2)
                for j in range(2):
                    last = flip(acc[use % 4][0:TS, 0, j * P:(j + 1) * P], qs_f[:, j, :])
                last.then_inc(acc_done, 1)
                use = T[f"s{h}"]
                free(use)
                for t in range(4):
                    for e in range(2):
                        for n, (q, k) in enumerate(((0, 0), (0, 1), (1, 0))):
                            last = M.matmul(acc[use % 4][:, t // 2, (t % 2) * N_MEM:(t % 2 + 1) * N_MEM],
                                            q_hl[q][:, e, t * P:(t + 1) * P], kT[k][:, 2 * h + e, :],
                                            start=e == 0 and n == 0, stop=e == 1 and n == 2)
                last.then_inc(acc_done, 1)
            head_tail(3)
            use = T["ss"]
            free(use)
            pe.wait_ge(acc_read, T["qb3"] + 2)
            for m in range(2):
                last = flip(acc[use % 4][0:NH * TS, 0, m * P:(m + 1) * P], sc[:, m, :])
            last.then_inc(acc_done, 1)
            use = T["sp"]
            free(use)
            pe.wait_ge(acc_read, T["ss"] + 1)
            for m in range(2):
                last = flip(acc[use % 4][:, 0, m * NH * TS:(m + 1) * NH * TS], p32[:, m * P:(m + 1) * P])
            last.then_inc(acc_done, 1)

            pe.wait_ge(acc_read, T["sp"] + 1)
            with pe.Fori(0, 2) as i:
                for j in range(4):
                    t0 = T["cx"] + 3 * j
                    chunk(i * 4 + (C_CX + j), j % 2, i * 12 + t0, t0, xn)
                    free(i * 12 + (t0 + 2))
                    pe.wait_ge(v_loaded[j % 2], i * 32 + 16 * (j // 2 + 1))
                    for e in range(2):
                        for s in range(4):
                            for m in range(2):
                                col = i * 2 + (m * NH * TS + (4 * (j % 2) + s) * NH + j // 2)
                                last = M.matmul(acc[(t0 + 2) % 4][:, 0, e * 4 + s:e * 4 + s + 1],
                                                v_st[:, j % 2, 2 * s + m, e * P:(e + 1) * P],
                                                flat(pT)[:, bass.ds(col, 1)], start=m == 0, stop=m == 1)
                    last.then_inc(acc_done, 1)
            use = T["ctail"]
            free(use)
            pe.wait_ge(u_used, 1 + KT)
            flip8_back(use, lambda k: ua_tail[:, k, :], slice(0, TS + 2), TS + 2)

            pairs(T["x"], C_X, (xn, br))
            for j in range(4):
                chunk(C_BA + j, j % 2, T["ba"] + 2 * j, T["ba"] + 2 * j, xn)
            pe.wait_ge(ba_lo, KT)
            pairs(T["a"], C_A, (xn, br))

            def mean(use, src):
                free(use)
                for b in range(2):
                    last = M.matmul(acc[use % 4][:, b, 0:HALF], ones[:, 0:1].broadcast_to([P, P]),
                                    src[:, b * HALF:(b + 1) * HALF], start=True, stop=True)
                last.then_inc(acc_done, 1)

            gb = T["gb"]
            pe.wait_ge(const_made, 2)
            chunk(C_GB, 0, gb, gb, xn)
            pe.wait_ge(ln_step, KT - 1)
            mean(gb + 2, ubyb[:, KT, :])
            chunk(C_GB + 1, 1, gb + 3, gb + 3, xn)
            chunk(C_GB + 2, 0, gb + 5, gb + 5, xn)
            pe.wait_ge(ln_acc, KT - 1)
            mean(gb + 7, ubyb[:, KT, :])
            chunk(C_GB + 3, 1, gb + 8, gb + 8, xn)

            pe.wait_ge(z_lo, KT)
            for j in range(4):
                chunk(C_OB + j, j % 2, T["ob"] + 2 * j, T["ob"] + 2 * j, zb)

            pe.wait_ge(m_lo, KT)
            for c in range(4):
                for j in range(2):
                    use = T["wo"] + 2 * c + j
                    free(use)
                    tile(c % 2, j, use, br, stop=False,
                         first_half=None if j else (lambda s: 2 * (C_WO + c) + s + 1))
                if c == 0:
                    pe.wait_ge(x_again, 16 * 5)
                for j in range(2):
                    use = T["wo"] + 2 * c + j
                    cols = slice((2 * c + j) * P, (2 * c + j + 1) * P)
                    for t in range(4):
                        for b in range(2):
                            a, z = max(t * P, b * HALF), min((t + 1) * P, (b + 1) * HALF)
                            if a < z:
                                M.matmul(acc[use % 4][:, b, a - b * HALF:z - b * HALF], x_st[:, t, cols],
                                         ident[:, a - t * P:z - t * P], start=False, stop=b == 0 and z == HALF)
                    M.matmul(acc[use % 4][:, 1, HALF - TS:HALF], xs_st[:, cols], ident[0:TS, 0:TS],
                             start=False, stop=True).then_inc(acc_done, 1)
            pe.wait_ge(h_sum, KT)
            mean(T["r"], hsum)

            pe.wait_ge(acc_read, T["wo"] + KT)
            with pe.Fori(0, FT // 2) as i:
                for j in range(2):
                    chunk(i * 2 + (C_F + j), j, i * 4 + (T["f"] + 2 * j), T["f"] + 2 * j, hg)

            pe.wait_ge(f_lo, FT + 2)

            def rows_out(p):
                for j in range(2):
                    use, n = T[f"y{p}"] + j, 2 * p + j
                    free(use)
                    pe.wait_ge(acc_read, T[f"d{p}"] + j + 1)
                    for t in range(4):
                        flip(acc[use % 4][:, 0, t * P:(t + 1) * P], h_sb[:, n, t * P:(t + 1) * P])
                    flip(acc[use % 4][0:TS, 1, 0:P], h_sb[:, n, TP:TOK]).then_inc(acc_done, 1)

            for p in range(4):
                for g, (k0, kn) in enumerate(((0, 8), (8, 8), (16, 6))):
                    c = C_D + 3 * p + g
                    for j in range(2):
                        use = T[f"d{p}"] + j
                        if g == 0:
                            free(use)
                        last = tile(c % 2, j, use, mid, k0, kn, start=g == 0, stop=g == 2,
                                    first_half=None if j else (lambda s: 2 * c + s + 1))
                        if g == 2:
                            last.then_inc(acc_done, 1)
                        elif j:
                            last.then_inc(d_used, 1)
                    if p and g == 0:
                        rows_out_later = p - 1
                if p:
                    rows_out(p - 1)
            rows_out(3)


_INS = ["x_prompt", "x_sample", "mem_prompt", "cache_mem_k", "cache_mem_v", "state_conv_a",
        "state_conv_b", "norm_mix", "w_in", "b_gate", "conv_a_w", "w_out_a", "conv_b_w",
        "conv_b_bias", "ln_b_g", "ln_b_b", "w_out_b", "norm_mem", "w_k", "w_v", "w_out_x", "w_o",
        "norm_ffn", "w_ff_gate", "w_ff_up", "w_ff_down", "norm_final"]
_OUTS = [(1, TP, D), (TS, 1, D), (1, 1, N_MEM, NH, DH), (1, 1, N_MEM, NH, DH), (1, 1, K_A - 1, D),
         (1, 1, K_B - 1, D), (1, TS, K_A - 1, D), (1, TS, K_B - 1, D)]


def kernel(**inputs):
    import numpy as _np
    import concourse.bacc as _bacc
    from concourse import mybir as _mybir
    from concourse.bass_utils import run_bass_kernel_spmd as _run

    nc = _bacc.Bacc("TRN2", target_bir_lowering=False, num_devices=1)
    arrays, args = {}, []
    for name in _INS:
        a = _np.ascontiguousarray(inputs[name])
        arrays[f"in_{name}_dram"] = a
        args.append(nc.dram_tensor(f"in_{name}_dram", a.shape, _mybir.dt.from_np(a.dtype), kind="ExternalInput").ap())
    for i, shape in enumerate(_OUTS):
        args.append(nc.dram_tensor(f"out_{i}_dram", shape, _mybir.dt.float32, kind="ExternalOutput").ap())
    decoder_step(nc, *args)
    r = _run(nc, [arrays], core_ids=[0])
    return tuple(r.results[0][f"out_{i}_dram"] for i in range(len(_OUTS)))
```

```python
from contextlib import ExitStack

import numpy as np
import concourse.bass as bass
from concourse import mybir

P = 128
D = 1024
KT = D // P
TP, TS = 512, 8
TOK = TP + TS
HALF = TOK // 2
N_MEM, NH, DH = 256, 4, 256
K_A, K_B = 3, 31
D_FF = 2816
FT = D_FF // P
CW = 256
HK = KT // 2
EPS = 1e-6
BATCHES = ((0, 2), (2, 4), (4, 7))
PAD = K_B - 1
SLOT = PAD + TOK
SG = 2 + TOK

COL_AB, COL_AC, COL_AX, COL_BV, COL_BG, COL_Q, COL_GATE = (n * D for n in range(7))
BR_A, BR_B, BR_X = range(3)

(R_MEM, R_MIX, R_BG, R_CA, R_CB, R_CBIAS, R_LNG, R_LNB, R_FFN, R_ALL) = (
    0, 1, 2, 5, 8, 39, 40, 41, 42, 43)

C_KV, C_B, C_Q, C_CX, C_X, C_BA, C_A, C_GB, C_OB, C_WO, C_F, C_D, C_END = (
    0, 8, 16, 20, 28, 36, 40, 48, 52, 56, 60, 82, 94)


def number_uses():
    T, n = {}, 0

    def use(name, count=1):
        nonlocal n
        T[name] = n
        n += count

    use("param")
    use("mem", 2)
    for c in range(8):
        use(f"kv{c}")
        if 1 <= c <= NH:
            use(f"kt{c - 1}")
        use(f"prep{c}")
    use("b", 16)
    for h in range(NH):
        use(f"q{h}0")
        if h:
            use(f"pt{h - 1}")
        use(f"q{h}1")
        if h == 0:
            use("btail")
        if h:
            use(f"o{h - 1}")
            use(f"qb{h - 1}0")
            use(f"qb{h - 1}1")
        use(f"qt{h}")
        use(f"s{h}")
    use("c0")
    use("qb30")
    use("pt3")
    use("c1")
    use("qb31")
    use("o3")
    use("cx", 24)
    T["ss"], T["sp"] = T["cx"], T["cx"] + 1
    use("x", 16)
    use("ba", 8)
    use("ctail")
    use("a", 16)
    use("gb", 10)
    use("ob", 8)
    use("wo", 8)
    use("fg", 2)
    use("r")
    use("fu", 2)
    use("f", 2 * FT - 4)
    for name in ("d0", "d1", "y0", "d2", "y1", "y2", "d3", "y3"):
        use(name, 2)
    return T


def decoder_step(nc, x_prompt, x_sample, mem_prompt, cache_mem_k, cache_mem_v, state_conv_a,
                 state_conv_b, norm_mix, w_in, b_gate, conv_a_w, w_out_a, conv_b_w, conv_b_bias,
                 ln_b_g, ln_b_b, w_out_b, norm_mem, w_k, w_v, w_out_x, w_o, norm_ffn, w_ff_gate,
                 w_ff_up, w_ff_down, norm_final, y_prompt, y_sample, mem_k_out, mem_v_out,
                 conv_a_prompt, conv_b_prompt, conv_a_sample, conv_b_sample):
    f32, f32r = mybir.dt.float32, mybir.dt.float32r
    ALU, ACT, AX = mybir.AluOpType, mybir.ActivationFunctionType, mybir.AxisListType
    T = number_uses()

    def chunks(w):
        return w.rearrange("(k p) n -> p k n", p=P)

    win = chunks(w_in[0])
    wk = chunks(w_k[0].rearrange("d h e -> d (h e)"))
    wv = chunks(w_v[0].rearrange("d h e -> d (h e)"))
    woa, wob, wox, wo = (chunks(w[0]) for w in (w_out_a, w_out_b, w_out_x, w_o))
    wfg, wfu, wfd = (chunks(w[0]) for w in (w_ff_gate, w_ff_up, w_ff_down))
    kcache, vcache = (c[0].rearrange("s m h e -> (s m) (h e)").rearrange("(a p) c -> p a c", p=P)
                      for c in (cache_mem_k, cache_mem_v))
    kout, vout = (o[0, 0].rearrange("m h e -> m (h e)").rearrange("(t p) c -> p t c", p=P)
                  for o in (mem_k_out, mem_v_out))
    xs_dram = x_sample.rearrange("s t d -> (s t) d")
    sa_dram = state_conv_a[0].rearrange("s j d -> (s j) d")
    sb_dram = state_conv_b[0].rearrange("s j d -> (s j) d")
    SB_ROWS = TS * PAD // 2

    base = -(-nc.sbuf_base // 32) * 32
    used = {}

    def align(off):
        return -(-off // 32) * 32

    def at(name, shape, dt, off):
        size = 4 * int(np.prod(shape[1:]))
        used[name] = off + size
        return nc.alloc_sbuf_tensor_at(name, shape, dt, offset=base + off)

    CH_B = KT * CW * 4
    o_raw, o_wh, o_wl = 0, 2 * CH_B, 4 * CH_B
    o_bh = 6 * CH_B
    ACTV = KT * TOK
    BIG = 3 * ACTV
    o_bl = o_bh + 4 * BIG
    o_ub = o_bl + 4 * BIG
    o_mg = align(o_ub + 4 * (KT + 1) * SLOT)
    o_h = o_mg + 4 * ACTV
    o_sm = o_h + 4 * ACTV
    w_raw = at("w_raw", [P, 2, KT, CW], f32, o_raw)
    w_h = at("w_h", [P, 2, KT, CW], f32r, o_wh)
    w_l = at("w_l", [P, 2, KT, CW], f32r, o_wl)
    big_h = at("big_h", [P, BIG], f32r, o_bh)
    big_l = at("big_l", [P, BIG], f32r, o_bl)

    def part(big, n, words=ACTV, inner=TOK, skip=0):
        return big[:, n * ACTV + skip:n * ACTV + skip + words].rearrange("p (k t) -> p k t", t=inner)

    xn = [part(b, 0) for b in (big_h, big_l)]
    br = [part(b, 1) for b in (big_h, big_l)]
    zb = [part(b, 2) for b in (big_h, big_l)]
    mn = [part(b, 1, KT * N_MEM, N_MEM) for b in (big_h, big_l)]
    kT = [part(b, 2, KT * N_MEM, N_MEM) for b in (big_h, big_l)]
    vM = [part(b, 2, 2 * D, D, KT * N_MEM) for b in (big_h, big_l)]
    mid = [b[:, 0:FT * TOK].rearrange("p (k t) -> p k t", t=TOK) for b in (big_h, big_l)]
    mid_f = [b[:, 0:FT * TOK] for b in (big_h, big_l)]
    o_p2h, o_p2l = o_bh + 8 * ACTV, o_bl + 8 * ACTV
    x_st = at("x_st", [P, 4, D], f32, o_p2h)
    nrm_2 = at("nrm_2", [P, KT, P], f32, o_p2h)
    xs_st = at("xs_st", [TS, D], f32, o_p2l)
    hsum = at("hsum", [P, TOK], f32, o_p2l + 4 * D)
    tail = 4 * FT * TOK
    rms = at("rms", [P, TOK], f32, o_bh + tail)
    sgf = at("sgf", [P, 2, TOK], f32, o_bl + tail)
    ubyb = at("ubyb", [P, KT + 1, SLOT], f32, o_ub)
    merged = at("merged", [P, KT, TOK], f32, o_mg)
    yA = at("yA", [P, KT, TOK], f32, o_h)
    sgB = at("sgB", [P, KT, TOK], f32, o_h)
    h_sb = at("h_sb", [P, KT, TOK], f32, o_h)
    stage = [at(f"stage{n}", [P, D], f32, o_ub + 4 * D * n if n < 8 else o_h + 4 * D * (n - 6))
             for n in range(10)]
    prow = at("prow", [R_ALL, D], f32, o_h)
    kv_f = at("kv_f", [P, 2, 2, CW], f32, o_h + 4 * D)
    q_hl = [at(f"q_{n}", [P, 2, TOK], f32r, o_h + 8 * TOK * i) for i, n in enumerate("hl")]
    pt_hl = [at(f"pt_{n}", [P, 2, TP], f32r, o_h + 16 * TOK + 8 * TP * i) for i, n in enumerate("hl")]
    p32 = at("p32", [NH * TS, N_MEM], f32, o_h)
    k_st = at("k_st", [P, 2 * TS, DH], f32, o_mg)
    v_st = at("v_st", [P, 2, TS, DH], f32, o_mg)
    uao = at("uao", [TS + 2, D], f32, o_p2h)
    hg = [at(f"hg_{n}", [P, KT, TOK], f32r, o_ub + 4 * ACTV * i) for i, n in enumerate("hl")]
    y_st = at("y_st", [P, 4, D], f32, o_ub)
    ys_st = at("ys_st", [TS, D], f32, o_ub + 16 * D)
    gfin = at("gfin", [P, D], f32, o_ub + 20 * D)
    junk = at("junk", [P, D], f32, o_ub + 24 * D)
    o = o_sm
    sg = at("sg", [P, 2, SG], f32, o)
    p_f = at("p_f", [P, 4, N_MEM], f32, o)
    nrm_t = at("nrm_t", [P, KT, P], f32, o)
    ubo = at("ubo", [PAD + TS, D], f32, o)
    o = align(o + 8 * SG)
    qs_hl = [at(f"qs_{n}", [TS, DH], f32r, o + 4 * DH * i) for i, n in enumerate("hl")]
    o += 8 * DH
    ident = at("ident", [P, P], f32, o)
    o += 4 * P
    prm = at("prm", [P, KT, R_ALL], f32, o)
    o += 4 * KT * R_ALL
    ysb = at("ysb", [P, KT, TS], f32, o)
    o += 4 * KT * TS
    ysa = at("ysa", [P, KT, TS], f32, o)
    o += 4 * KT * TS
    ua_tail = at("ua_tail", [P, KT, TS + 2], f32, o)
    o += 4 * KT * (TS + 2)
    qs_f = at("qs_f", [P, 2, TS], f32, o)
    o += 64
    sc = at("sc", [P, 2, NH * TS], f32, o)
    o += 256
    pT = at("pT", [P, 2, NH * TS], f32, o)
    o += 256
    ident_r = at("ident_r", [TS, TS], f32r, o)
    o += 32
    ones = at("ones", [P, 8], f32, o)
    eps = ones[:, 4:5]
    o += 32
    st = at("st", [P, 64], f32, o)
    o += 256
    ss, rs_, mx, nb, rsum, rrec = (st[:, a:b] for a, b in ((0, 8), (8, 16), (16, 20), (20, 24), (24, 28), (28, 32)))
    mx32, nb32, rsum32, rrec32 = (st[0:NH * TS, 32 + n:33 + n] for n in range(4))
    ssy, rfin, t_ = st[:, 36:51], st[:, 51:56], st[:, 56:64]
    assert base + o <= nc.sbuf_usable_end, (base + o, nc.sbuf_usable_end)
    junk_norm = at("junk_norm", [P, D], f32, o_bh + 4 * (ACTV + KT * N_MEM))

    def flat(t):
        return t[:, :, :].rearrange("p a b -> p (a b)")

    prm_f, ubyb_f, merged_f, yA_f = flat(prm), flat(ubyb), flat(merged), flat(yA)

    def param(tile, row):
        if isinstance(tile, int):
            return prm[:, tile, row:row + 1]
        return prm_f[:, bass.ds(tile * R_ALL + row, 1)]

    ctx = ExitStack()
    with ctx:
        acc = [ctx.enter_context(nc.psum_tensor(f"acc{n}", [P, 2, 512], f32)) for n in range(4)]

        def sem(name):
            return ctx.enter_context(nc.semaphore(name))

        acc_done = sem("acc_done")
        acc_read = sem("acc_read")
        w_loaded = [sem("w_loaded0"), sem("w_loaded1")]
        w_hi = sem("w_hi")
        w_lo = sem("w_lo")
        row_in = [sem(f"row_in{n}") for n in range(10)]
        prow_in = sem("prow_in")
        const_made = sem("const_made")
        ident_made = sem("ident_made")
        stats_clear = sem("stats_clear")
        table_loaded = sem("table_loaded")
        refined = sem("refined")
        sumsq = sem("sumsq")
        meansq = sem("meansq")
        rootsq = sem("rootsq")
        row_scaled = sem("row_scaled")
        nrm_hi = sem("nrm_hi")
        nrm_lo = sem("nrm_lo")
        kv_hi = sem("kv_hi")
        kv_lo = sem("kv_lo")
        kv_stored = [sem("kv_stored0"), sem("kv_stored1")]
        state_sum = sem("state_sum")
        pads = sem("pads")
        b_sig = sem("b_sig")
        ubo_stored = sem("ubo_stored")
        q_hi = sem("q_hi")
        at_hi = sem("at_hi")
        at_exp = sem("at_exp")
        at_max = sem("at_max")
        at_step = sem("at_step")
        k_loaded = [sem("k_loaded0"), sem("k_loaded1")]
        v_loaded = [sem("v_loaded0"), sem("v_loaded1")]
        k_used = sem("k_used")
        ss_max = sem("ss_max")
        ss_exp = sem("ss_exp")
        ss_step = sem("ss_step")
        cv_step = sem("cv_step")
        cs_step = sem("cs_step")
        c_copied = sem("c_copied")
        u_used = sem("u_used")
        ca_step = sem("ca_step")
        v_hi = sem("v_hi")
        uao_stored = sem("uao_stored")
        x_sig = sem("x_sig")
        ba_hi = sem("ba_hi")
        ba_lo = sem("ba_lo")
        a_sig = sem("a_sig")
        a_step = sem("a_step")
        gb_sig = sem("gb_sig")
        ln_step = sem("ln_step")
        ln_sub = sem("ln_sub")
        ln_sq = sem("ln_sq")
        ln_acc = sem("ln_acc")
        ln_root = sem("ln_root")
        z_aff = sem("z_aff")
        z_sig = sem("z_sig")
        z_f = sem("z_f")
        z_hi = sem("z_hi")
        z_lo = sem("z_lo")
        m_sum = sem("m_sum")
        m_hi = sem("m_hi")
        m_lo = sem("m_lo")
        x_again = sem("x_again")
        h_hi = sem("h_hi")
        h_sq = sem("h_sq")
        h_sum = sem("h_sum")
        r_root = sem("r_root")
        f_sig = sem("f_sig")
        f_step = sem("f_step")
        f_hi = sem("f_hi")
        f_lo = sem("f_lo")
        d_used = sem("d_used")
        y_sq = sem("y_sq")
        y_step = sem("y_step")
        y_root = sem("y_root")
        y_out = sem("y_out")
        g_in = sem("g_in")
        stored = sem("stored")

        block = ctx.enter_context(nc.Block())

        def halves(use):
            return acc[use % 4][:, :, 0:HALF]

        z_tmp = [ubyb[:, KT, 0:TOK], sg[:, 0, 0:TOK]]

        def two(ap):
            return ap.rearrange("p (h t) -> p h t", h=2)

        def f(ap):
            return ap.bitcast(f32)

        @block.sync
        def _(sp):
            def load(c, slot, src, col, k0=0, kn=KT):
                if not isinstance(c, int):
                    sp.wait_ge(w_lo, c * 2 - 2)
                elif c >= 2:
                    sp.wait_ge(w_lo, 2 * c - 2)
                sp.dma_start(w_raw[:, slot, 0:kn, :], src[:, k0:k0 + kn, bass.ds(col, CW)]) \
                    .then_inc(w_loaded[slot], 16)

            for n in range(2):
                sp.dma_start(stage[n][:, :], mem_prompt[0, n * P:(n + 1) * P, :]).then_inc(row_in[n], 16)
            sp.dma_start(prow[R_CB:R_CB + K_B, :], conv_b_w[0]).then_inc(prow_in, 16)
            sp.dma_start(prow[R_CA:R_CA + K_A, :], conv_a_w[0]).then_inc(prow_in, 16)
            sp.dma_start(prow[R_BG:R_BG + 3, :], b_gate[0].rearrange("(b d) -> b d", d=D)).then_inc(prow_in, 16)
            sp.dma_start(prow[R_LNG:R_LNG + 1, :], ln_b_g).then_inc(prow_in, 16)
            sp.dma_start(prow[R_LNB:R_LNB + 1, :], ln_b_b).then_inc(prow_in, 16)
            load(0, 0, wk, 0)
            load(1, 1, wk, CW)
            for n in range(4):
                sp.dma_start(stage[2 + n][:, :], x_prompt[0, n * P:(n + 1) * P, :]).then_inc(row_in[2 + n], 16)
            sp.dma_start(stage[6][0:TS, :], xs_dram).then_inc(row_in[6], 16)
            for n in range(2):
                sp.dma_start(stage[7 + n][0:SB_ROWS, :], sb_dram[n * SB_ROWS:(n + 1) * SB_ROWS, :]) \
                    .then_inc(row_in[7 + n], 16)
            sp.dma_start(stage[9][0:2 * TS, :], sa_dram).then_inc(row_in[9], 16)
            for c in range(2, 8):
                load(c, c % 2, wk if c < 4 else wv, (c % 4) * CW)
            sp.dma_start(conv_b_sample[0, :, 0:PAD - 1, :], state_conv_b[0, :, 1:PAD, :]).then_inc(stored, 16)
            sp.dma_start(conv_a_sample[0, :, 0:1, :], state_conv_a[0, :, 1:2, :]).then_inc(stored, 16)

            def pairs(c0, bodies, sources):
                with sp.Fori(0, bodies) as i:
                    for j in range(4):
                        src, col = sources[j % 2]
                        load(i * 4 + (c0 + j), j % 2, src, i * (2 * CW) + (col + (j // 2) * CW))

            pairs(C_B, 2, ((win, COL_BG), (win, COL_BV)))
            for j in range(4):
                load(C_Q + j, j % 2, win, COL_Q + j * CW)
            pairs(C_CX, 2, ((win, COL_AC), (win, COL_AX)))
            for j in range(8):
                load(C_X + j, j % 2, *((wox, j // 2 * CW) if j % 2 else (win, COL_GATE + BR_X * D + j // 2 * CW)))
            for j in range(4):
                load(C_BA + j, j % 2, win, COL_AB + j * CW)
            for j in range(8):
                load(C_A + j, j % 2, *((woa, j // 2 * CW) if j % 2 else (win, COL_GATE + BR_A * D + j // 2 * CW)))
            for j in range(4):
                load(C_GB + j, j % 2, win, COL_GATE + BR_B * D + j * CW)
            for j in range(4):
                load(C_OB + j, j % 2, wob, j * CW)
            for j in range(4):
                load(C_WO + j, j % 2, wo, j * CW)
            with sp.Fori(0, FT // 2) as i:
                load(i * 2 + C_F, 0, wfg, i * CW)
                load(i * 2 + (C_F + 1), 1, wfu, i * CW)
            for p in range(4):
                for g, (k0, kn) in enumerate(((0, 8), (8, 8), (16, 6))):
                    load(C_D + 3 * p + g, (3 * p + g) % 2, wfd, p * CW, k0, kn)
            sp.wait_ge(stored, 16 * 2)
            for s in range(2):
                sp.wait_ge(kv_stored[s], 16 * 4)
            sp.wait_ge(ubo_stored, 32)
            sp.wait_ge(uao_stored, 32)
            sp.wait_ge(y_out, 16 * 5)

        @block.gpsimd
        def _(pool):
            nc.gpsimd.memset(ident[:, :], 0.0).then_inc(ident_made, 1)
            nc.gpsimd.memset(ones[:, 0:4], 1.0 / D).then_inc(const_made, 1)
            nc.gpsimd.memset(ones[:, 4:8], EPS).then_inc(const_made, 1)
            nc.gpsimd.memset(st[:, :], 1.0).then_inc(stats_clear, 1)
            pool.wait_ge(ident_made, 1)
            nc.gpsimd.affine_select(out=ident[:, :], in_=ident[:, :], compare_op=ALU.not_equal, fill=1.0,
                                    base=0, pattern=[[-1, P]], channel_multiplier=1).then_inc(ident_made, 1)
            pool.wait_ge(ident_made, 2)
            nc.gpsimd.tensor_copy(ident_r[:, :], ident[0:TS, 0:TS]).then_inc(ident_made, 1)
            with pool.Fori(0, C_END // 2) as i:
                for j in range(2):
                    for s in range(2):
                        pool.wait_ge(w_hi, i * 4 + (2 * j + s + 1))
                        ks = slice(s * HK, (s + 1) * HK)
                        nc.gpsimd.tensor_tensor(w_l[:, j, ks, :], w_raw[:, j, ks, :], f(w_h[:, j, ks, :]),
                                                ALU.subtract).then_inc(w_lo, 1)

        @block.scalar
        def _(act):
            def done(use):
                act.wait_ge(acc_done, use + 1)

            def hi_part(slot):
                for s in range(2):
                    ks = slice(s * HK, (s + 1) * HK)
                    nc.scalar.activation(w_h[:, slot, ks, :], w_raw[:, slot, ks, :], ACT.Copy).then_inc(w_hi, 1)

            def split(c, slot, last_use=None):
                act.wait_ge(w_loaded[slot], (c // 2 + 1) * 16)
                if last_use is not None:
                    done(last_use)
                hi_part(slot)

            def split_in_loop(i, per_body, c0, j, last_use):
                act.wait_ge(w_loaded[j % 2], i * (8 * per_body) + 16 * ((c0 + j) // 2 + 1))
                done(last_use)
                hi_part(j % 2)

            act.wait_ge(stats_clear, 1)
            nc.scalar.activation(rfin[:, 0:1], rfin[:, 0:1], ACT.Sqrt).then_inc(table_loaded, 1)

            for w, row in ((norm_mem, R_MEM), (norm_mix, R_MIX), (norm_ffn, R_FFN),
                           (conv_b_bias, R_CBIAS)):
                act.dma_start(prow[row:row + 1, :], w).then_inc(prow_in, 16)


            def squares(n, rows):
                act.wait_ge(row_in[n], 16)
                act.wait_ge(sumsq, n)
                nc.scalar.activation(junk_norm[0:rows, :], stage[n][0:rows, :], ACT.Square,
                                     accum_out=ss[0:rows, n:n + 1]).then_inc(sumsq, 1)

            act.wait_ge(meansq, 1)
            nc.scalar.activation(rs_[:, 0:2], ss[:, 0:2], ACT.Sqrt).then_inc(rootsq, 1)

            def norm_tile(use, dst, cols, rows, src=nrm_t):
                act.wait_ge(acc_read, use + 1)
                nc.scalar.activation(dst[:, :, cols], src[:, :, 0:rows], ACT.Copy).then_inc(nrm_hi, 1)

            split(0, 0)
            norm_tile(T["mem"], mn[0], slice(0, P), P)
            norm_tile(T["mem"] + 1, mn[0], slice(P, 2 * P), P, nrm_2)
            split(1, 1)
            for batch, (a, b) in enumerate(BATCHES[1:]):
                for n in range(a, b):
                    squares(n, TS if n == 6 else P)
                act.wait_ge(meansq, batch + 2)
                nc.scalar.activation(rs_[:, a:b], ss[:, a:b], ACT.Sqrt).then_inc(rootsq, 1)

            for c in range(8):
                use = T[f"kv{c}"]
                if c >= 1:
                    split(c + 1, (c + 1) % 2, T[f"kv{c - 1}"])
                    if c < 6:
                        rows = P if c < 5 else TS
                        norm_tile(T[f"prep{c - 1}"], xn[0], slice((c - 1) * P, (c - 1) * P + rows), rows)
                if c >= 4:
                    done(use)
                    nc.scalar.activation(vM[0][:, :, (c - 4) * CW:(c - 3) * CW], acc[use % 4][:, :, 0:CW],
                                         ACT.Copy).then_inc(kv_hi, 1)
                act.wait_ge(acc_read, use + 1)
                dst = kout if c < 4 else vout
                act.dma_start(dst[:, :, (c % 4) * CW:(c % 4 + 1) * CW], kv_f[:, c % 2, :, :]) \
                    .then_inc(kv_stored[c % 2], 16)
                if 1 <= c <= NH:
                    use = T[f"kt{c - 1}"]
                    done(use)
                    nc.scalar.activation(kT[0][:, 2 * (c - 1):2 * c, :], acc[use % 4][:, :, 0:N_MEM],
                                         ACT.Copy).then_inc(kv_hi, 1)

            def load_k(h, u):
                act.dma_start(k_st[:, u * TS:(u + 1) * TS, :], kcache[:, u * TS:(u + 1) * TS, h * DH:(h + 1) * DH]) \
                    .then_inc(k_loaded[u], 16)

            act.wait_ge(acc_read, T["b"])
            for u in range(2):
                load_k(0, u)
            act.wait_ge(state_sum, 3)

            with act.Fori(0, 2) as i:
                for p in range(2):
                    u0 = i * 8 + (T["b"] + 4 * p)
                    split_in_loop(i, 4, C_B, 2 * p + 1, u0 - 1)
                    for j in range(2):
                        done(u0 + j)
                        act.wait_ge(acc_read, u0)
                        nc.scalar.activation(two(sg[:, j, 2:SG]), halves(T["b"] + 4 * p + j), ACT.Sigmoid) \
                            .then_inc(b_sig, 1)
                    split_in_loop(i, 4, C_B, 2 * p + 2, u0 + 1)

            def probs_t(h):
                use = T[f"pt{h}"]
                done(use)
                nc.scalar.activation(pt_hl[0][:, :, :], acc[use % 4][:, :, :], ACT.Copy).then_inc(at_hi, 1)

            def out_t(h):
                use = T[f"o{h}"]
                done(use)
                nc.scalar.activation(br[0][:, 2 * h:2 * h + 2, 0:TP], acc[use % 4][:, :, :], ACT.Copy) \
                    .then_inc(at_hi, 1)

            for s in range(2):
                act.wait_ge(kv_stored[s], 16 * 4)
            def q_part(h, j):
                use = T[f"q{h}{j}"]
                done(use)
                if h and j == 0:
                    done(T[f"s{h - 1}"])
                nc.scalar.activation(two(q_hl[0][:, j, :]), halves(use), ACT.Copy).then_inc(q_hi, 1)

            for h in range(NH):
                split(C_Q + h + 1, (h + 1) % 2, T["b"] + 15 if h == 0 else T[f"q{h - 1}1"])
                q_part(h, 0)
                if h:
                    probs_t(h - 1)
                q_part(h, 1)
                if h == 0:
                    act.wait_ge(acc_read, T["btail"] + 1)
                    act.dma_start(conv_b_prompt[0, 0], ubo[0:PAD, :]).then_inc(ubo_stored, 16)
                    act.dma_start(conv_b_sample[0, :, PAD - 1, :], ubo[PAD:PAD + TS, :]).then_inc(ubo_stored, 16)
                if h:
                    out_t(h - 1)
                use = T[f"qt{h}"]
                done(use)
                nc.scalar.activation(qs_hl[0][:, :], acc[use % 4][0:TS, 0, 0:DH], ACT.Copy).then_inc(at_hi, 1)
                if h:
                    act.wait_ge(acc_read, T[f"qb{h - 1}0"] + 1)
                    load_k(h, 0)
                use = T[f"s{h}"]
                done(use)
                if h == 0:
                    act.wait_ge(ubo_stored, 32)
                act.wait_ge(at_max, h + 1)
                for t in range(4):
                    nc.scalar.activation(p_f[:, t, :], acc[use % 4][:, t // 2, (t % 2) * N_MEM:(t % 2 + 1) * N_MEM],
                                         ACT.Exp, bias=nb[:, t:t + 1], scale=DH ** -0.5,
                                         accum_out=rsum[:, t:t + 1]).then_inc(at_exp, 1)
                if h:
                    act.wait_ge(acc_read, T[f"qb{h - 1}1"] + 1)
                    load_k(h, 1)
            def load_v(q):
                h, n = divmod(q, 2)
                act.dma_start(v_st[:, n, :, :], vcache[:, n * TS:(n + 1) * TS, h * DH:(h + 1) * DH]) \
                    .then_inc(v_loaded[n], 16)

            def c_copy(n, use):
                done(use)
                nc.scalar.activation(two(sg[:, n, 2:SG]), halves(use), ACT.Copy).then_inc(c_copied, 1)

            split(C_CX + 1, 1, T["q31"])
            probs_t(3)
            c_copy(0, T["c0"])
            act.wait_ge(k_used, 1)
            load_v(0)
            c_copy(1, T["c1"])
            out_t(3)
            use = T["ss"]
            done(use)
            act.wait_ge(ss_max, 1)
            nc.scalar.activation(p32[:, :], acc[use % 4][0:NH * TS, 0, 0:N_MEM], ACT.Exp, bias=nb32,
                                 scale=DH ** -0.5, accum_out=rsum32).then_inc(ss_exp, 1)
            act.wait_ge(acc_read, T["qb31"] + 1)
            load_v(1)

            for q in range(8):
                u0 = T["cx"] + 3 * q
                if q:
                    split(C_CX + q + 1, (q + 1) % 2, u0 - 2 if q > 1 else T["c1"])
                if q and q % 2 == 0:
                    act.wait_ge(u_used, q + 1)
                    for n in range(2):
                        c_copy(n, u0 + n)
                use = u0 + 2
                done(use)
                h, n = divmod(q, 2)
                nc.scalar.activation(br[0][:, 2 * h:2 * h + 2, TP + 4 * n:TP + 4 * n + 4],
                                     acc[use % 4][:, 0, 0:8].rearrange("p (e s) -> p e s", e=2),
                                     ACT.Copy).then_inc(v_hi, 1)
                if q + 2 < 8:
                    load_v(q + 2)

            def gate_stage(t0, c0, row, sig):
                with act.Fori(0, 2) as i:
                    for p in range(2):
                        u0 = i * 8 + (t0 + 4 * p)
                        split_in_loop(i, 4, c0, 2 * p + 1, u0 - 1)
                        for j in range(2):
                            done(u0 + j)
                            act.wait_ge(acc_read, u0)
                            nc.scalar.activation(two(sg[:, j, 2:SG]), halves(t0 + 4 * p + j), ACT.Sigmoid,
                                                 bias=param(i * 4 + (2 * p + j), row)).then_inc(sig, 1)
                        split_in_loop(i, 4, c0, 2 * p + 2, u0 + 1)

            act.wait_ge(u_used, 1 + KT)
            gate_stage(T["x"], C_X, R_BG + BR_X, x_sig)

            for n in range(KT):
                if n % 2 == 0:
                    split(C_BA + n // 2 + 1, (n // 2 + 1) % 2, T["ba"] + n - 1)
                act.wait_ge(acc_read, T["ba"] + n + 1)
                nc.scalar.activation(br[0][:, n, :], yA[:, n, :], ACT.Copy).then_inc(ba_hi, 1)

            act.wait_ge(acc_read, T["ctail"] + 1)
            act.dma_start(conv_a_prompt[0, 0], uao[0:2, :]).then_inc(uao_stored, 16)
            act.dma_start(conv_a_sample[0, :, 1, :], uao[2:2 + TS, :]).then_inc(uao_stored, 16)

            gate_stage(T["a"], C_A, R_BG + BR_A, a_sig)

            def gate_b(n, use):
                if n == 2:
                    split(C_GB + n // 2 + 1, (n // 2 + 1) % 2, use - 1)
                done(use)
                if n == 0:
                    act.wait_ge(ba_lo, KT)
                nc.scalar.activation(two(sgB[:, n, :]), halves(use), ACT.Sigmoid,
                                     bias=prm[:, n, R_BG + BR_B:R_BG + BR_B + 1]).then_inc(gb_sig, 1)

            def ln_square(k):
                act.wait_ge(ln_sub, k + 1)
                if k >= 2:
                    act.wait_ge(ln_acc, k - 1)
                nc.scalar.activation(sg[:, k % 2, 0:TOK], ubyb[:, k, 0:TOK], ACT.Square).then_inc(ln_sq, 1)

            def z_sigmoid(k):
                act.wait_ge(z_aff, k + 1)
                if k >= 2:
                    act.wait_ge(z_f, k - 1)
                nc.scalar.activation(z_tmp[k % 2], ubyb[:, k, 0:TOK], ACT.Sigmoid, bias=param(k, R_LNB)) \
                    .then_inc(z_sig, 1)

            def z_hi_part(k):
                act.wait_ge(z_f, k + 1)
                if k == 0:
                    act.wait_ge(uao_stored, 32)
                nc.scalar.activation(zb[0][:, k, :], ubyb[:, k, 0:TOK], ACT.Copy).then_inc(z_hi, 1)

            gb = T["gb"]
            split(C_GB + 1, 1, gb - 1)
            for k in range(4):
                ln_square(k)
            gate_b(0, gb + 1)
            for k in range(4, 8):
                ln_square(k)
            gate_b(1, gb + 2)
            gate_b(2, gb + 3)
            gate_b(3, gb + 4)
            split(C_GB + 3, 1, gb + 4)
            done(gb + 5)
            nc.scalar.activation(two(sg[:, 1, 0:TOK]), halves(gb + 5), ACT.Sqrt, bias=eps).then_inc(ln_root, 1)
            z_sigmoid(0)
            for k in range(1, KT):
                z_sigmoid(k)
                z_hi_part(k - 1)
                if k in (2, 4, 6):
                    gate_b(4 + k // 2 - 1, gb + 6 + k // 2 - 1)
                if k == 4:
                    split(C_OB, 0, gb + 7)
            z_hi_part(KT - 1)
            gate_b(7, gb + 9)

            for n in range(KT):
                if n % 2 == 0:
                    split(C_OB + n // 2 + 1, (n // 2 + 1) % 2, T["ob"] + n - 1)
                act.wait_ge(m_sum, n + 1)
                nc.scalar.activation(br[0][:, n, :], merged[:, n, :], ACT.Copy).then_inc(m_hi, 1)

            done(T["ob"] + 7)
            for t in range(4):
                act.dma_start(x_st[:, t, :], x_prompt[0, t * P:(t + 1) * P, :]).then_inc(x_again, 16)
            act.dma_start(xs_st[:, :], xs_dram).then_inc(x_again, 16)

            for n in range(KT):
                if n % 2 == 0:
                    split(C_WO + n // 2 + 1, (n // 2 + 1) % 2, T["wo"] + n - 1)
                use = T["wo"] + n
                done(use)
                if n >= 2:
                    act.wait_ge(h_sum, n - 1)
                nc.scalar.activation(two(sg[:, n % 2, 0:TOK]), halves(use), ACT.Square).then_inc(h_sq, 1)
                if n == 0:
                    act.wait_ge(m_lo, KT)
                nc.scalar.activation(two(hg[0][:, n, :]), halves(use), ACT.Copy,
                                     scale=prm[:, n, R_FFN:R_FFN + 1]).then_inc(h_hi, 1)
            def middle(i, u_gate, u_up, root=False):
                split_next(i, 1, u_gate - 1)
                if root:
                    done(T["r"])
                    nc.scalar.activation(two(rms[:, :]), halves(T["r"]), ACT.Sqrt, bias=eps).then_inc(r_root, 1)
                for j in range(2):
                    act.wait_ge(acc_read, u_gate + (j + 1))
                    nc.scalar.activation(sgf[:, j, :], sg[:, j, 0:TOK], ACT.Sigmoid).then_inc(f_sig, 1)
                split_next(i, 2, u_gate + 1)
                for j in range(2):
                    act.wait_ge(acc_read, u_up + (1 + j))
                    nc.scalar.activation(mid_f[0][:, bass.ds(i * (2 * TOK) + j * TOK, TOK)], sg[:, j, 0:TOK],
                                         ACT.Copy).then_inc(f_hi, 1)

            def split_next(i, j, last_use):
                split_in_loop(i, 2, C_F, j, last_use)

            middle(0, T["fg"], T["fu"], root=True)
            with act.Fori(1, FT // 2) as i:
                u0 = i * 4 + (T["f"] - 4)
                middle(i, u0, u0 + 2)

            act.wait_ge(acc_read, T["d0"])
            act.dma_start(gfin[:, :], norm_final.rearrange("(a d) -> a d", a=1).broadcast_to([P, D])) \
                .then_inc(g_in, 16)
            for c in range(C_D + 1, C_END):
                p, g = divmod(c - 2 - C_D, 3)
                if c == C_D + 1:
                    done(T["d0"] - 1)
                elif g == 2:
                    done(T[f"d{p}"] + 1)
                else:
                    act.wait_ge(d_used, 2 * p + g + 1)
                act.wait_ge(w_loaded[c % 2], (c // 2 + 1) * 16)
                hi_part(c % 2)
            y_cols = ((0, 6 * P, T["y2"] + 2), (6 * P, 7 * P, T["y3"] + 1), (7 * P, D, T["y3"] + 2))
            n = 0
            for part_n, (a, b, read) in enumerate(y_cols):
                act.wait_ge(acc_read, read)
                for t in range(5):
                    src = y_st[:, t, a:b] if t < 4 else ys_st[:, a:b]
                    rows = P if t < 4 else TS
                    if n:
                        act.wait_ge(y_sq, n)
                    nc.scalar.activation(junk[0:rows, 0:b - a], src, ACT.Square,
                                         accum_out=ssy[0:rows, 5 * part_n + t:5 * part_n + t + 1]).then_inc(y_sq, 1)
                    n += 1
                if part_n == 0:
                    nc.scalar.activation(t_[:, 0:1], t_[:, 1:2], ACT.Sqrt).then_inc(table_loaded, 1)
            act.wait_ge(y_step, 2)
            nc.scalar.activation(rfin[:, :], ssy[:, 0:5], ACT.Sqrt).then_inc(y_root, 1)
            for t in range(5):
                act.wait_ge(y_step, 3 + t)
                if t < 4:
                    act.dma_start(y_prompt[0, t * P:(t + 1) * P, :], y_st[:, t, :]).then_inc(y_out, 16)
                else:
                    act.dma_start(y_sample.rearrange("s t d -> (s t) d"), ys_st[:, :]).then_inc(y_out, 16)

        @block.vector
        def _(dve):
            V = nc.vector

            def done(use):
                dve.wait_ge(acc_done, use + 1)

            dve.wait_ge(stats_clear, 1)

            steps = 0

            def step(ins):
                nonlocal steps
                ins.then_inc(refined, 1)
                steps += 1
                dve.wait_ge(refined, steps)

            def refine(v, root, t, r):
                step(V.reciprocal(r, root))
                step(V.tensor_tensor(t, r, r, ALU.mult))
                step(V.tensor_tensor(t, t, v, ALU.mult))
                step(V.tensor_scalar(t, t, -0.5, 1.5, ALU.mult, ALU.add))
                step(V.tensor_tensor(r, r, t, ALU.mult))

            for n in range(2):
                dve.wait_ge(row_in[n], 16)
                if n:
                    dve.wait_ge(sumsq, 1)
                V.scalar_tensor_tensor(junk_norm[:, :], stage[n][:, :], 1.0, stage[n][:, :], ALU.mult, ALU.mult,
                                       accum_out=ss[:, n:n + 1]).then_inc(sumsq, 1)

            def norm_rows(batch, a, b):
                dve.wait_ge(sumsq, b)
                V.tensor_scalar(ss[:, a:b], ss[:, a:b], 1.0 / D, EPS, ALU.mult, ALU.add).then_inc(meansq, 1)
                dve.wait_ge(meansq, batch + 1)
                dve.wait_ge(rootsq, batch + 1)
                refine(ss[:, a:b], rs_[:, a:b], t_[:, a:b], rs_[:, a:b])
                for n in range(a, b):
                    rows = TS if n == 6 else P
                    V.tensor_scalar(stage[n][0:rows, :], stage[n][0:rows, :], rs_[0:rows, n:n + 1], None,
                                    ALU.mult).then_inc(row_scaled, 1)

            def blocks(use, rows):
                return acc[use % 4][:, :, :].rearrange("p b (k r) -> p (b k) r", r=P)[:, :, 0:rows]

            norm_rows(0, *BATCHES[0])
            done(T["param"])
            V.tensor_copy(prm[:, :, :], blocks(T["param"], R_ALL)).then_inc(acc_read, 1)
            dve.wait_ge(acc_read, 1)
            lo_count = 0

            def norm_gain(use, gain_row, rows, buf):
                done(use)
                V.tensor_tensor(buf[:, :, 0:rows], blocks(use, rows),
                                prm[:, :, gain_row:gain_row + 1].broadcast_to([P, KT, rows]),
                                ALU.mult).then_inc(acc_read, 1)

            def norm_lo(dst, cols, rows, buf):
                nonlocal lo_count
                lo_count += 1
                dve.wait_ge(nrm_hi, lo_count)
                V.tensor_tensor(dst[1][:, :, cols], buf[:, :, 0:rows], f(dst[0][:, :, cols]),
                                ALU.subtract).then_inc(nrm_lo, 1)

            bufs = (nrm_t, nrm_2)
            for n in range(2):
                norm_gain(T["mem"] + n, R_MEM, P, bufs[n])
            for n in range(2):
                norm_lo(mn, slice(n * P, (n + 1) * P), P, bufs[n])
            for batch in (1, 2):
                norm_rows(batch, *BATCHES[batch])

            hi_count = 0
            for c in range(8):
                use = T[f"kv{c}"]
                done(use)
                if c >= 4:
                    hi_count += 1
                    dve.wait_ge(kv_hi, hi_count)
                    cols = slice((c - 4) * CW, (c - 3) * CW)
                    V.tensor_tensor(vM[1][:, :, cols], acc[use % 4][:, :, 0:CW], f(vM[0][:, :, cols]),
                                    ALU.subtract).then_inc(kv_lo, 1)
                if c >= 2:
                    dve.wait_ge(kv_stored[c % 2], 16 * (c // 2))
                V.tensor_copy(kv_f[:, c % 2, :, :], acc[use % 4][:, :, 0:CW]).then_inc(acc_read, 1)
                if 1 <= c <= NH:
                    use = T[f"kt{c - 1}"]
                    done(use)
                    hi_count += 1
                    dve.wait_ge(kv_hi, hi_count)
                    V.tensor_tensor(kT[1][:, 2 * c - 2:2 * c, :], acc[use % 4][:, :, 0:N_MEM],
                                    f(kT[0][:, 2 * c - 2:2 * c, :]), ALU.subtract).then_inc(acc_read, 1)
                use = T[f"prep{c}"]
                if c < 5:
                    rows = P if c < 4 else TS
                    dve.wait_ge(nrm_lo, lo_count)
                    norm_gain(use, R_MIX, rows, nrm_t)
                    norm_lo(xn, slice(c * P, c * P + rows), rows, nrm_t)
                    continue
                done(use)
                taps, row, samples = (PAD, R_CB, TS // 2) if c < 7 else (K_A - 1, R_CA, TS)
                prod = nrm_t[:, :, 0:samples * taps].rearrange("p k (s j) -> p k s j", j=taps)
                w = prm[:, :, row:row + taps].rearrange("p k (s j) -> p k s j", s=1) \
                    .broadcast_to([P, KT, samples, taps])
                if c > 5:
                    dve.wait_ge(state_sum, c - 5)
                else:
                    dve.wait_ge(nrm_lo, lo_count)
                V.tensor_tensor(prod, blocks(use, samples * taps).rearrange("p k (s j) -> p k s j", j=taps), w,
                                ALU.mult).then_inc(acc_read, 1)
                dve.wait_ge(acc_read, use + 1)
                dst = ysb[:, :, (c - 5) * samples:(c - 4) * samples] if c < 7 else ysa[:, :, :]
                V.tensor_reduce(dst, prod, AX.X, ALU.add).then_inc(state_sum, 1)
            dve.wait_ge(state_sum, 3)
            V.tensor_tensor(ysb[:, :, :], ysb[:, :, :],
                            prm[:, :, R_CBIAS:R_CBIAS + 1].broadcast_to([P, KT, TS]), ALU.add).then_inc(state_sum, 1)
            V.memset(ubyb[:, 1:KT + 1, 0:PAD], 0.0).then_inc(pads, 1)

            def conv(tile, steps):
                y = ubyb_f[:, bass.ds(tile * SLOT, TP)]
                for k in steps:
                    if not isinstance(tile, int) or tile or k:
                        dve.wait_ge(cv_step, tile * K_B + min(k, K_B))
                    if k == K_B:
                        V.scalar_tensor_tensor(
                            ubyb_f[:, bass.ds(tile * SLOT + TP, TS)], ubyb_f[:, bass.ds(tile * SLOT + (SLOT + PAD + TP), TS)],
                            param(tile, R_CB + K_B - 1), flat(ysb)[:, bass.ds(tile * TS, TS)], ALU.mult, ALU.add) \
                            .then_inc(cs_step, 1)
                        continue
                    u = ubyb_f[:, bass.ds(tile * SLOT + (SLOT + k), TP)]
                    w = param(tile, R_CB + k)
                    if k == 0:
                        ins = V.tensor_scalar(y, u, w, param(tile, R_CBIAS), ALU.mult, ALU.add)
                    else:
                        ins = V.scalar_tensor_tensor(y, u, w, y, ALU.mult, ALU.add)
                    ins.then_inc(cv_step, 1)

            CV = K_B + 1
            Q4 = (range(0, 12), range(12, 16), range(16, 28), range(28, CV))

            dve.wait_ge(pads, 1)
            for i in range(2):
                for p in range(2):
                    u0 = T["b"] + 8 * i + 4 * p
                    if i + p:
                        dve.wait_ge(acc_read, T["b"] + 4)
                    if i == 0 and p == 1:
                        conv(0, range(20))
                    elif i and p == 0:
                        conv(0, range(20, K_B))
                        conv(1, range(9))
                    elif i:
                        conv(1, range(9, 29))
                    dve.wait_ge(b_sig, 4 * i + 2 * p + 2)
                    for j in range(2):
                        n = 4 * i + 2 * p + j
                        done(u0 + 2 + j)
                        V.tensor_tensor(two(ubyb[:, n + 1, PAD:SLOT]), halves(u0 + 2 + j), two(sg[:, j, 2:SG]),
                                        ALU.mult).then_inc(acc_read, 1 if j else 3)

            conv(1, range(29, K_B))

            dve.wait_ge(acc_read, T["b"] + 16)
            hi_count = 0

            def lo_part(use, dst, src, release=1):
                nonlocal hi_count
                hi_count += 1
                done(use)
                dve.wait_ge(at_hi, hi_count)
                ins = V.tensor_tensor(dst[1], src, f(dst[0]), ALU.subtract)
                if release:
                    ins.then_inc(acc_read, release)

            def q_lo(h, j):
                use = T[f"q{h}{j}"]
                done(use)
                dve.wait_ge(q_hi, 2 * h + j + 1)
                V.tensor_copy(qs_f[:, j, :], acc[use % 4][:, 1, HALF - TS:HALF])
                V.tensor_tensor(two(q_hl[1][:, j, :]), halves(use), two(f(q_hl[0][:, j, :])),
                                ALU.subtract).then_inc(acc_read, 1)

            def probs_lo(h, release=1):
                use = T[f"pt{h}"]
                lo_part(use, [q[:, :, :] for q in pt_hl], acc[use % 4][:, :, :], release)

            def out_lo(h, release=1):
                use = T[f"o{h}"]
                lo_part(use, [b[:, 2 * h:2 * h + 2, 0:TP] for b in br], acc[use % 4][:, :, :], release)

            def sample_scores(h, u):
                dve.wait_ge(k_loaded[u], 16 * (h + 1))
                use = T[f"qb{h}{u}"]
                done(use)
                for s in range(4):
                    for m in range(2):
                        a = (4 * u + s) * 2 + m
                        col = (4 * u + s) * NH + h
                        ins = V.scalar_tensor_tensor(
                            k_st[:, a, :], k_st[:, a, :], 1.0, acc[use % 4][:, s // 2, (s % 2) * DH:(s % 2 + 1) * DH],
                            ALU.mult, ALU.mult, accum_out=sc[:, m, col:col + 1])
                return ins

            def score_max(h):
                use = T[f"s{h}"]
                done(use)
                scores = acc[use % 4][:, :, :].rearrange("p b (t m) -> p (b t) m", m=N_MEM)
                V.reduce_max(mx[:, :], scores, AX.X).then_inc(at_step, 1)
                dve.wait_ge(at_step, 2 * h + 1)
                V.tensor_scalar(nb[:, :], mx[:, :], -(DH ** -0.5), None, ALU.mult).then_inc(at_max, 1)

            def normalise(h, release):
                dve.wait_ge(at_exp, 4 * h + 4)
                V.reciprocal(rrec[:, :], rsum[:, :]).then_inc(at_step, 1)
                dve.wait_ge(at_step, 2 * h + 2)
                V.tensor_tensor(p_f[:, :, :], p_f[:, :, :],
                                rrec[:, :].rearrange("p (t m) -> p t m", m=1).broadcast_to([P, 4, N_MEM]),
                                ALU.mult).then_inc(acc_read, release)

            taps = (0, 14, 20, 25, 25)
            for h in range(NH):
                if h == 0:
                    conv(2, range(0, 3))
                q_lo(h, 0)
                if h:
                    probs_lo(h - 1)
                conv(2, range(taps[h], taps[h + 1]) if h else range(3, 8))
                q_lo(h, 1)
                if h == 0:
                    done(T["btail"])
                    V.tensor_copy(ubo[:, :].rearrange("p (b c) -> p b c", b=2),
                                  acc[T["btail"] % 4][0:PAD + TS, :, :]).then_inc(acc_read, 1)
                    conv(0, [K_B])
                    conv(1, [K_B])
                if h:
                    out_lo(h - 1)
                    sample_scores(h - 1, 0).then_inc(acc_read, 1)
                use = T[f"qt{h}"]
                lo_part(use, [q[:, :] for q in qs_hl], acc[use % 4][0:TS, 0, 0:DH], 0)
                score_max(h)
                if h:
                    sample_scores(h - 1, 1).then_inc(acc_read, 1)
                else:
                    conv(2, range(8, 11))
                normalise(h, 2)
                if h == 0:
                    conv(2, range(11, taps[1]))
            sample_scores(3, 0).then_inc(k_used, 1)
            dve.wait_ge(c_copied, 1)
            probs_lo(3, 3)
            dve.wait_ge(c_copied, 2)
            sample_scores(3, 1).then_inc(acc_read, 2)
            use = T["ss"]
            done(use)
            V.reduce_max(mx32, acc[use % 4][0:NH * TS, 0, 0:N_MEM], AX.X).then_inc(ss_step, 1)
            dve.wait_ge(ss_step, 1)
            V.tensor_scalar(nb32, mx32, -(DH ** -0.5), None, ALU.mult).then_inc(ss_max, 1)
            out_lo(3)
            dve.wait_ge(ss_exp, 1)
            V.reciprocal(rrec32, rsum32).then_inc(ss_step, 1)
            dve.wait_ge(ss_step, 2)
            V.tensor_scalar(p32[:, :], p32[:, :], rrec32, None, ALU.mult).then_inc(ss_step, 1)
            use = T["sp"]
            done(use)
            V.tensor_copy(pT[:, :, :], acc[use % 4][:, 0, 0:2 * NH * TS].rearrange("p (m c) -> p m c", m=2)) \
                .then_inc(ss_step, 1)
            V.memset(sg[:, :, 0:2], 0.0).then_inc(u_used, 1)
            conv(2, range(taps[NH], CV))

            with dve.Fori(0, 2) as i:
                for p in range(2):
                    u0 = i * 12 + (T["cx"] + 6 * p)

                    def piece(n, use, static, release):
                        done(use)
                        dve.wait_ge(v_hi, i * 4 + (2 * p + n + 1))
                        cols = slice(TP + 4 * n, TP + 4 * n + 4)
                        h2 = bass.ds(i * 4 + 2 * p, 2)
                        V.tensor_tensor(br[1][:, h2, cols], acc[static % 4][:, 0, 0:8].rearrange("p (e s) -> p e s", e=2),
                                        f(br[0][:, h2, cols]), ALU.subtract).then_inc(acc_read, release)

                    dve.wait_ge(c_copied, i * 4 + (2 * p + 2))
                    piece(0, u0 + 2, T["cx"] + 6 * p + 2, 3)
                    conv(i + 3, Q4[2 * p][:6])
                    for j in range(2):
                        n = i * 4 + (2 * p + j)
                        done(u0 + (3 + j))
                        V.tensor_tensor(two(sg[:, j, 2:SG]), halves(T["cx"] + 6 * p + 3 + j), two(sg[:, j, 2:SG]),
                                        ALU.mult).then_inc(acc_read, 1)
                        dve.wait_ge(acc_read, u0 + (4 + j))
                        if j:
                            piece(1, u0 + 5, T["cx"] + 6 * p + 5, 1)
                        y = yA_f[:, bass.ds(n * TOK, TP)]
                        V.tensor_scalar(y, sg[:, j, 0:TP], param(n, R_CA), None, ALU.mult).then_inc(ca_step, 1)
                        V.scalar_tensor_tensor(yA_f[:, bass.ds(n * TOK + TP, TS)], sg[:, j, SG - TS:SG],
                                               param(n, R_CA + 2), flat(ysa)[:, bass.ds(n * TS, TS)], ALU.mult, ALU.add)
                        V.tensor_copy(flat(ua_tail)[:, bass.ds(n * (TS + 2), TS + 2)], sg[:, j, SG - TS - 2:SG])
                        for k in (1, 2):
                            dve.wait_ge(ca_step, i * 8 + (4 * p + 2 * j + k))
                            V.scalar_tensor_tensor(y, sg[:, j, k:k + TP], param(n, R_CA + k), y, ALU.mult, ALU.add) \
                                .then_inc(ca_step if k == 1 else u_used, 1)
                        conv(i + 3, Q4[2 * p][6:] if j == 0 else Q4[2 * p + 1])

            with dve.Fori(0, 2) as i:
                for p in range(2):
                    u0 = i * 8 + (T["x"] + 4 * p)
                    conv(i + 5, Q4[2 * p])
                    dve.wait_ge(x_sig, i * 4 + (2 * p + 2))
                    for j in range(2):
                        done(u0 + (2 + j))
                        dst = merged_f[:, bass.ds(i * (4 * TOK) + (2 * p + j) * TOK, TOK)]
                        V.tensor_tensor(two(dst), halves(T["x"] + 4 * p + 2 + j), two(sg[:, j, 2:SG]),
                                        ALU.mult).then_inc(acc_read, 1 if j else 3)
                        if j == 0:
                            conv(i + 5, Q4[2 * p + 1])

            def ba_lo_part(n):
                dve.wait_ge(ba_hi, n + 1)
                V.tensor_tensor(br[1][:, n, :], yA[:, n, :], f(br[0][:, n, :]), ALU.subtract).then_inc(ba_lo, 1)

            dve.wait_ge(u_used, 1 + KT)
            for n in range(KT):
                done(T["ba"] + n)
                V.tensor_tensor(two(yA[:, n, :]), halves(T["ba"] + n), two(yA[:, n, :]), ALU.mult) \
                    .then_inc(acc_read, 1)
                if n:
                    ba_lo_part(n - 1)
                conv(7, range(4 * n, 4 * n + 4))
            ba_lo_part(KT - 1)
            done(T["ctail"])
            V.tensor_copy(uao[:, :].rearrange("p (b c) -> p b c", b=2), acc[T["ctail"] % 4][0:TS + 2, :, :]) \
                .then_inc(acc_read, 1)

            dve.wait_ge(cs_step, KT)
            dve.wait_ge(cv_step, KT * K_B)
            total = ubyb[:, KT, 0:TOK]
            for k in range(1, KT):
                V.tensor_tensor(total, ubyb[:, k, 0:TOK], ubyb[:, 0, 0:TOK] if k == 1 else total, ALU.add) \
                    .then_inc(ln_step, 1)
                dve.wait_ge(ln_step, k)

            with dve.Fori(0, 2) as i:
                for p in range(2):
                    u0 = i * 8 + (T["a"] + 4 * p)
                    dve.wait_ge(a_sig, i * 4 + (2 * p + 2))
                    for j in range(2):
                        done(u0 + (2 + j))
                        V.tensor_tensor(two(sg[:, j, 2:SG]), halves(T["a"] + 4 * p + 2 + j), two(sg[:, j, 2:SG]),
                                        ALU.mult).then_inc(a_step, 1)
                        dve.wait_ge(a_step, i * 4 + (2 * p + j + 1))
                        dst = merged_f[:, bass.ds(i * (4 * TOK) + (2 * p + j) * TOK, TOK)]
                        V.tensor_tensor(dst, dst, sg[:, j, 2:SG], ALU.add).then_inc(acc_read, 1 if j else 3)

            gb = T["gb"]

            def gates_read(n):
                dve.wait_ge(gb_sig, n + 2)
                V.memset(mx[:, n // 2:n // 2 + 1], 0.0).then_inc(acc_read, 2)

            done(gb)
            for k in range(KT):
                ins = V.tensor_tensor(two(ubyb[:, k, 0:TOK]), two(ubyb[:, k, 0:TOK]), halves(gb), ALU.subtract)
                ins.then_inc(ln_sub, 1)
            dve.wait_ge(ln_sq, 1)
            V.tensor_copy(total, sg[:, 0, 0:TOK]).then_inc(acc_read, 1)
            dve.wait_ge(acc_read, gb + 1)
            for k in range(1, KT):
                dve.wait_ge(ln_sq, k + 1)
                V.tensor_tensor(total, total, sg[:, k % 2, 0:TOK], ALU.add).then_inc(ln_acc, 1)
                dve.wait_ge(ln_acc, k)
            gates_read(0)
            gates_read(2)
            done(gb + 5)
            dve.wait_ge(ln_root, 1)
            V.reciprocal(sg[:, 1, 0:TOK], sg[:, 1, 0:TOK]).then_inc(acc_read, 1)
            dve.wait_ge(acc_read, gb + 6)

            def affine(k):
                V.scalar_tensor_tensor(ubyb[:, k, 0:TOK], ubyb[:, k, 0:TOK], param(k, R_LNG), sg[:, 1, 0:TOK],
                                       ALU.mult, ALU.mult).then_inc(z_aff, 1)

            def z_lo_part(k):
                dve.wait_ge(z_hi, k + 1)
                V.tensor_tensor(zb[1][:, k, :], ubyb[:, k, 0:TOK], f(zb[0][:, k, :]), ALU.subtract) \
                    .then_inc(z_lo, 1)

            dve.wait_ge(ln_sub, KT)
            affine(0)
            for k in range(KT):
                if k + 1 < KT:
                    affine(k + 1)
                dve.wait_ge(z_sig, k + 1)
                V.scalar_tensor_tensor(ubyb[:, k, 0:TOK], ubyb[:, k, 0:TOK], param(k, R_LNB), z_tmp[k % 2],
                                       ALU.add, ALU.mult).then_inc(z_f, 1)
                if k:
                    z_lo_part(k - 1)
                if k == 5:
                    gates_read(4)
            z_lo_part(KT - 1)

            def m_lo_part(n):
                dve.wait_ge(m_hi, n + 1)
                V.tensor_tensor(br[1][:, n, :], merged[:, n, :], f(br[0][:, n, :]), ALU.subtract).then_inc(m_lo, 1)

            dve.wait_ge(gb_sig, KT)
            for n in range(KT):
                done(T["ob"] + n)
                V.tensor_tensor(two(sgB[:, n, :]), halves(T["ob"] + n), two(sgB[:, n, :]), ALU.mult) \
                    .then_inc(acc_read, 1 if n else 3)
                dve.wait_ge(acc_read, T["ob"] + n + 1)
                V.tensor_tensor(merged[:, n, :], merged[:, n, :], sgB[:, n, :], ALU.add).then_inc(m_sum, 1)
                if n:
                    m_lo_part(n - 1)
            m_lo_part(KT - 1)

            for n in range(KT):
                use = T["wo"] + n
                done(use)
                dve.wait_ge(h_hi, n + 1)
                V.tensor_copy(two(h_sb[:, n, :]), halves(use))
                if n == 0:
                    V.tensor_copy(hsum[:, :], sg[:, 0, 0:TOK]).then_inc(h_sum, 1)
                else:
                    dve.wait_ge(h_sum, n)
                    V.tensor_tensor(hsum[:, :], hsum[:, :], sg[:, n % 2, 0:TOK], ALU.add).then_inc(h_sum, 1)
                V.scalar_tensor_tensor(two(hg[1][:, n, :]), halves(use), param(n, R_FFN), two(f(hg[0][:, n, :])),
                                       ALU.mult, ALU.subtract).then_inc(acc_read, 1)

            def middle(i, u_gate, u_up, gate, up, release):
                for j in range(2):
                    done(u_gate + j)
                    dve.wait_ge(f_lo, i * 2 + (j + 1))
                    V.tensor_tensor(two(sg[:, j, 0:TOK]), halves(gate + j), two(rms[:, :]), ALU.mult) \
                        .then_inc(acc_read, release if j else 1)
                for j in range(2):
                    dve.wait_ge(f_sig, i * 2 + (j + 1))
                    V.tensor_tensor(sg[:, j, 0:TOK], sg[:, j, 0:TOK], sgf[:, j, :], ALU.mult).then_inc(f_step, 1)
                for j in range(2):
                    dve.wait_ge(f_step, i * 4 + (j + 1))
                    V.tensor_tensor(sg[:, j, 0:TOK], sg[:, j, 0:TOK], rms[:, :], ALU.mult).then_inc(f_step, 1)
                for j in range(2):
                    done(u_up + j)
                    dve.wait_ge(f_step, i * 4 + (j + 3))
                    V.tensor_tensor(two(sg[:, j, 0:TOK]), halves(up + j), two(sg[:, j, 0:TOK]), ALU.mult) \
                        .then_inc(acc_read, 1)
                for j in range(2):
                    dve.wait_ge(f_hi, i * 2 + (j + 1))
                    cols = bass.ds(i * (2 * TOK) + j * TOK, TOK)
                    V.tensor_tensor(mid_f[1][:, cols], sg[:, j, 0:TOK], f(mid_f[0][:, cols]), ALU.subtract) \
                        .then_inc(f_lo, 1)

            dve.wait_ge(h_sum, KT)
            dve.wait_ge(r_root, 1)
            V.reciprocal(rms[:, :], rms[:, :]).then_inc(f_lo, 2)
            dve.wait_ge(f_lo, 2)
            middle(0, T["fg"], T["fu"], T["fg"], T["fu"], 2)
            with dve.Fori(1, FT // 2) as i:
                u0 = i * 4 + (T["f"] - 4)
                middle(i, u0, u0 + 2, T["f"], T["f"] + 2, 1)

            def rows_out(p):
                for j in range(2):
                    use = T[f"y{p}"] + j
                    cols = slice((2 * p + j) * P, (2 * p + j + 1) * P)
                    done(use)
                    V.tensor_copy(y_st[:, :, cols], acc[use % 4][:, 0, :].rearrange("p (t c) -> p t c", c=P))
                    V.tensor_copy(ys_st[:, cols], acc[use % 4][0:TS, 1, 0:P]).then_inc(acc_read, 1)

            for p in range(4):
                for j in range(2):
                    n, use = 2 * p + j, T[f"d{p}"] + j
                    done(use)
                    V.tensor_tensor(two(h_sb[:, n, :]), halves(use), two(h_sb[:, n, :]), ALU.add) \
                        .then_inc(acc_read, 1)
                for q in ((), (0,), (1, 2), (3,))[p]:
                    rows_out(q)
            dve.wait_ge(y_sq, 15)
            V.tensor_reduce(rfin[:, :], ssy.rearrange("p (c t) -> p t c", c=3), AX.X, ALU.add).then_inc(y_step, 1)
            dve.wait_ge(y_step, 1)
            V.tensor_scalar(ssy[:, 0:5], rfin[:, :], 1.0 / D, EPS, ALU.mult, ALU.add).then_inc(y_step, 1)
            dve.wait_ge(y_step, 2)
            dve.wait_ge(y_root, 1)
            refine(ssy[:, 0:5], rfin[:, :], ssy[:, 5:10], rfin[:, :])
            dve.wait_ge(g_in, 16)
            for t in range(5):
                rows = P if t < 4 else TS
                y = y_st[:, t, :] if t < 4 else ys_st[:, :]
                V.scalar_tensor_tensor(y, y, rfin[0:rows, t:t + 1], gfin[0:rows, :], ALU.mult, ALU.mult) \
                    .then_inc(y_step, 1)

        @block.tensor
        def _(pe):
            M = nc.tensor

            def free(use):
                if not isinstance(use, int) or use >= 4:
                    pe.wait_ge(acc_read, use - 3)

            def flip(out, src):
                rows = src.shape[0]
                return M.transpose(out, src, ident[0:rows, 0:rows])

            def flip8(use, src, rows):
                for k in range(KT):
                    last = flip(acc[use % 4][:, k // 4, (k % 4) * P:(k % 4) * P + rows], src[0:rows, k * P:(k + 1) * P])
                last.then_inc(acc_done, 1)

            def flip8_back(use, src, cols, count):
                for k in range(KT):
                    last = flip(acc[use % 4][0:count, k // 4, (k % 4) * P:(k % 4 + 1) * P], src(k)[:, cols])
                last.then_inc(acc_done, 1)

            def weights(half):
                pe.wait_ge(w_lo, half)

            def tile(slot, j, use, x, k_at=0, ks=KT, start=True, stop=True, first_half=None,
                     ready=None, beside=None):
                out = acc[use % 4]
                for k in range(ks):
                    if ready is not None:
                        pe.wait_ge(ready[0], ready[1] + k + 1)
                    if first_half is not None and k % HK == 0:
                        weights(first_half(k // HK))
                    cols = slice(j * P, (j + 1) * P)
                    wh, wl = w_h[:, slot, k, cols], w_l[:, slot, k, cols]
                    for w, xs in ((wh, x[0]), (wh, x[1]), (wl, x[0])):
                        for b in range(2):
                            last = M.matmul(out[:, b, 0:HALF], w, xs[:, k_at + k, b * HALF:(b + 1) * HALF],
                                            start=start and k == 0 and w is wh and xs is x[0],
                                            stop=stop and k == ks - 1 and w is wl)
                    if beside is not None and k < ks - 1:
                        beside(k)
                return last

            def chunk(c, slot, use, static, x, ready=None):
                for j in range(2):
                    free(use + j)
                    tile(slot, j, static + j, x, ready=None if j else ready,
                         first_half=None if j else (lambda s: c * 2 + (s + 1))).then_inc(acc_done, 1)

            pe.wait_ge(ident_made, 3)
            pe.wait_ge(prow_in, 16 * 9)
            flip8(T["param"], prow, R_ALL)
            for n in range(2):
                pe.wait_ge(row_scaled, n + 1)
                flip8(T["mem"] + n, stage[n], P)

            for c in range(8):
                use = T[f"kv{c}"]
                free(use)
                for m in range(2):
                    if c == 0:
                        pe.wait_ge(nrm_lo, m + 1)
                    for k in range(KT):
                        if m == 0 and k % HK == 0:
                            weights(2 * c + k // HK + 1)
                        rows = slice(m * P, (m + 1) * P)
                        for n, (x, w) in enumerate(((mn[0], w_h), (mn[0], w_l), (mn[1], w_h))):
                            last = M.matmul(acc[use % 4][:, m, 0:CW], x[:, k, rows], w[:, c % 2, k, :],
                                            start=k == 0 and n == 0, stop=k == KT - 1 and n == 2)
                last.then_inc(acc_done, 1)
                if 1 <= c <= NH:
                    use = T[f"kt{c - 1}"]
                    free(use)
                    pe.wait_ge(acc_read, T[f"kv{c - 1}"] + 1)
                    for e in range(2):
                        for m in range(2):
                            last = flip(acc[use % 4][:, e, m * P:(m + 1) * P],
                                        kv_f[:, (c - 1) % 2, m, e * P:(e + 1) * P])
                    last.then_inc(acc_done, 1)
                use = T[f"prep{c}"]
                free(use)
                if c < 5:
                    pe.wait_ge(row_scaled, c + 3)
                else:
                    pe.wait_ge(row_in[c + 2], 16)
                flip8(use, stage[c + 2], (P, P, P, P, TS, SB_ROWS, SB_ROWS, 2 * TS)[c])

            pe.wait_ge(nrm_lo, 7)

            def pairs(t0, c0, xs, ready=None):
                with pe.Fori(0, 2) as i:
                    for j in range(4):
                        if j == 1 and ready is not None:
                            pe.wait_ge(*ready)
                        chunk(i * 4 + (c0 + j), j % 2, i * 8 + (t0 + 2 * j), t0 + 2 * j, xs[j % 2])

            pairs(T["b"], C_B, (xn, xn))

            def q_tile(h, j):
                use = T[f"q{h}{j}"]
                free(use)
                tile(h % 2, j, use, xn,
                     first_half=None if j else (lambda s: 2 * (C_Q + h) + s + 1)).then_inc(acc_done, 1)

            def probs_t(h):
                use = T[f"pt{h}"]
                free(use)
                pe.wait_ge(acc_read, T[f"s{h}"] + 1)
                for t in range(4):
                    for m in range(2):
                        last = flip(acc[use % 4][:, m, t * P:(t + 1) * P], p_f[:, t, m * P:(m + 1) * P])
                last.then_inc(acc_done, 1)

            def sample_rows(h, u):
                pe.wait_ge(at_max, h + 1)
                use = T[f"qb{h}{u}"]
                free(use)
                for s in range(4):
                    row = ident_r[:, 4 * u + s:4 * u + s + 1].broadcast_to([TS, P])
                    for n in range(2):
                        last = M.matmul(acc[use % 4][:, s // 2, (s % 2) * DH:(s % 2 + 1) * DH], row,
                                        qs_hl[n][:, :], start=n == 0, stop=n == 1)
                last.then_inc(acc_done, 1)

            def out_t(h):
                use = T[f"o{h}"]
                free(use)
                if h == 0:
                    pe.wait_ge(kv_lo, 4)
                pe.wait_ge(acc_read, T[f"pt{h}"] + 1)
                for e in range(2):
                    for m in range(2):
                        cols = slice(h * DH + e * P, h * DH + (e + 1) * P)
                        for n, (v, p) in enumerate(((0, 0), (0, 1), (1, 0))):
                            last = M.matmul(acc[use % 4][:, e, :], vM[v][:, m, cols], pt_hl[p][:, m, :],
                                            start=m == 0 and n == 0, stop=m == 1 and n == 2)
                last.then_inc(acc_done, 1)

            for h in range(NH):
                q_tile(h, 0)
                if h:
                    probs_t(h - 1)
                q_tile(h, 1)
                if h == 0:
                    use = T["btail"]
                    free(use)
                    pe.wait_ge(acc_read, T["b"] + 16)
                    flip8_back(use, lambda k: ubyb[:, k + 1, :], slice(SLOT - TS - PAD, SLOT), PAD + TS)
                if h:
                    out_t(h - 1)
                    sample_rows(h - 1, 0)
                    sample_rows(h - 1, 1)
                use = T[f"qt{h}"]
                free(use)
                pe.wait_ge(acc_read, T[f"q{h}1"] + 1)
                for j in range(2):
                    last = flip(acc[use % 4][0:TS, 0, j * P:(j + 1) * P], qs_f[:, j, :])
                last.then_inc(acc_done, 1)
                use = T[f"s{h}"]
                free(use)
                for t in range(4):
                    for e in range(2):
                        for n, (q, k) in enumerate(((0, 0), (0, 1), (1, 0))):
                            last = M.matmul(acc[use % 4][:, t // 2, (t % 2) * N_MEM:(t % 2 + 1) * N_MEM],
                                            q_hl[q][:, e, t * P:(t + 1) * P], kT[k][:, 2 * h + e, :],
                                            start=e == 0 and n == 0, stop=e == 1 and n == 2)
                last.then_inc(acc_done, 1)
            free(T["c0"])
            tile(0, 0, T["c0"], xn, first_half=lambda s: 2 * C_CX + s + 1).then_inc(acc_done, 1)
            sample_rows(3, 0)
            probs_t(3)
            free(T["c1"])
            tile(0, 1, T["c1"], xn).then_inc(acc_done, 1)
            sample_rows(3, 1)
            out_t(3)
            use = T["ss"]
            free(use)
            pe.wait_ge(acc_read, T["qb31"] + 1)
            for m in range(2):
                last = flip(acc[use % 4][0:NH * TS, 0, m * P:(m + 1) * P], sc[:, m, :])
            last.then_inc(acc_done, 1)
            use = T["sp"]
            free(use)
            pe.wait_ge(ss_step, 3)
            for m in range(2):
                last = flip(acc[use % 4][:, 0, m * NH * TS:(m + 1) * NH * TS], p32[:, m * P:(m + 1) * P])
            last.then_inc(acc_done, 1)

            pe.wait_ge(ss_step, 4)
            for q in range(8):
                u0, (h, half) = T["cx"] + 3 * q, divmod(q, 2)

                def sample_out(k, u0=u0, h=h, half=half):
                    e, s = k // 4, k % 4
                    for m in range(2):
                        col = (4 * half + s) * NH + h
                        last = M.matmul(acc[(u0 + 2) % 4][:, 0, k:k + 1], v_st[:, half, 2 * s + m, e * P:(e + 1) * P],
                                        pT[:, m, col:col + 1], start=m == 0, stop=m == 1)
                    return last

                if q == 0:
                    free(u0 + 2)
                    pe.wait_ge(v_loaded[0], 16)
                    piece_0 = sample_out
                    continue
                weights_of = lambda s, q=q: 2 * (C_CX + q) + s + 1
                free(u0)
                if q == 1:
                    def beside(k):
                        for n in ((), (), (), (0, 1), (2, 3), (4, 5), (6, 7))[k]:
                            last = piece_0(n)
                            if n == KT - 1:
                                last.then_inc(acc_done, 1)
                    tile(half, 0, u0, xn, first_half=weights_of, beside=beside).then_inc(acc_done, 1)
                else:
                    tile(half, 0, u0, xn, first_half=weights_of).then_inc(acc_done, 1)
                free(u0 + 2)
                pe.wait_ge(v_loaded[half], 16 * (h + 1))
                tile(half, 1, u0 + 1, xn, beside=sample_out).then_inc(acc_done, 1)
                sample_out(KT - 1).then_inc(acc_done, 1)

            pairs(T["x"], C_X, (xn, br), (acc_read, T["x"]))
            for j in range(4):
                chunk(C_BA + j, j % 2, T["ba"] + 2 * j, T["ba"] + 2 * j, xn)
            use = T["ctail"]
            free(use)
            pe.wait_ge(u_used, 1 + KT)
            flip8_back(use, lambda k: ua_tail[:, k, :], slice(0, TS + 2), TS + 2)
            pairs(T["a"], C_A, (xn, br), (ba_lo, KT))

            def mean(use, src):
                free(use)
                for b in range(2):
                    last = M.matmul(acc[use % 4][:, b, 0:HALF], ones[:, 0:1].broadcast_to([P, P]),
                                    src[:, b * HALF:(b + 1) * HALF], start=True, stop=True)
                last.then_inc(acc_done, 1)

            gb = T["gb"]
            pe.wait_ge(const_made, 2)
            pe.wait_ge(ln_step, KT - 1)
            mean(gb, ubyb[:, KT, :])
            chunk(C_GB, 0, gb + 1, gb + 1, xn)
            chunk(C_GB + 1, 1, gb + 3, gb + 3, xn)
            pe.wait_ge(ln_acc, KT - 1)
            mean(gb + 5, ubyb[:, KT, :])
            chunk(C_GB + 2, 0, gb + 6, gb + 6, xn)
            chunk(C_GB + 3, 1, gb + 8, gb + 8, xn)

            for j in range(4):
                chunk(C_OB + j, j % 2, T["ob"] + 2 * j, T["ob"] + 2 * j, zb, None if j else (z_lo, 0))

            for c in range(4):
                for j in range(2):
                    use = T["wo"] + 2 * c + j
                    free(use)
                    tile(c % 2, j, use, br, stop=False, ready=None if c + j else (m_lo, 0),
                         first_half=None if j else (lambda s: 2 * (C_WO + c) + s + 1))
                if c == 0:
                    pe.wait_ge(x_again, 16 * 5)
                for j in range(2):
                    use = T["wo"] + 2 * c + j
                    cols = slice((2 * c + j) * P, (2 * c + j + 1) * P)
                    for t in range(4):
                        for b in range(2):
                            a, z = max(t * P, b * HALF), min((t + 1) * P, (b + 1) * HALF)
                            if a < z:
                                M.matmul(acc[use % 4][:, b, a - b * HALF:z - b * HALF], x_st[:, t, cols],
                                         ident[:, a - t * P:z - t * P], start=False, stop=b == 0 and z == HALF)
                    M.matmul(acc[use % 4][:, 1, HALF - TS:HALF], xs_st[:, cols], ident[0:TS, 0:TS],
                             start=False, stop=True).then_inc(acc_done, 1)

            chunk(C_F, 0, T["fg"], T["fg"], hg, (acc_read, T["wo"]))
            pe.wait_ge(h_sum, KT)
            mean(T["r"], hsum)
            chunk(C_F + 1, 1, T["fu"], T["fu"], hg)
            with pe.Fori(1, FT // 2) as i:
                for j in range(2):
                    chunk(i * 2 + (C_F + j), j, i * 4 + (T["f"] + 2 * j - 4), T["f"] + 2 * j, hg)

            def rows_out(p):
                for j in range(2):
                    use, n = T[f"y{p}"] + j, 2 * p + j
                    free(use)
                    pe.wait_ge(acc_read, T[f"d{p}"] + j + 1)
                    for t in range(4):
                        flip(acc[use % 4][:, 0, t * P:(t + 1) * P], h_sb[:, n, t * P:(t + 1) * P])
                    flip(acc[use % 4][0:TS, 1, 0:P], h_sb[:, n, TP:TOK]).then_inc(acc_done, 1)

            for p in range(4):
                if p == 3:
                    rows_out(2)
                for g, (k0, kn) in enumerate(((0, 8), (8, 8), (16, 6))):
                    c = C_D + 3 * p + g
                    if p == 0:
                        pe.wait_ge(f_lo, k0 + kn + 2)
                    for j in range(2):
                        use = T[f"d{p}"] + j
                        if g == 0:
                            free(use)
                        last = tile(c % 2, j, use, mid, k0, kn, start=g == 0, stop=g == 2,
                                    first_half=None if j else (lambda s: 2 * c + s + 1))
                        if g == 2:
                            last.then_inc(acc_done, 1)
                        elif j:
                            last.then_inc(d_used, 1)
                if p in (1, 2):
                    rows_out(p - 1)
            rows_out(3)


_INS = ["x_prompt", "x_sample", "mem_prompt", "cache_mem_k", "cache_mem_v", "state_conv_a",
        "state_conv_b", "norm_mix", "w_in", "b_gate", "conv_a_w", "w_out_a", "conv_b_w",
        "conv_b_bias", "ln_b_g", "ln_b_b", "w_out_b", "norm_mem", "w_k", "w_v", "w_out_x", "w_o",
        "norm_ffn", "w_ff_gate", "w_ff_up", "w_ff_down", "norm_final"]
_OUTS = [(1, TP, D), (TS, 1, D), (1, 1, N_MEM, NH, DH), (1, 1, N_MEM, NH, DH), (1, 1, K_A - 1, D),
         (1, 1, K_B - 1, D), (1, TS, K_A - 1, D), (1, TS, K_B - 1, D)]


def kernel(**inputs):
    import numpy as _np
    import concourse.bacc as _bacc
    from concourse import mybir as _mybir
    from concourse.bass_utils import run_bass_kernel_spmd as _run

    nc = _bacc.Bacc("TRN2", target_bir_lowering=False, num_devices=1)
    arrays, args = {}, []
    for name in _INS:
        a = _np.ascontiguousarray(inputs[name])
        arrays[f"in_{name}_dram"] = a
        args.append(nc.dram_tensor(f"in_{name}_dram", a.shape, _mybir.dt.from_np(a.dtype), kind="ExternalInput").ap())
    for i, shape in enumerate(_OUTS):
        args.append(nc.dram_tensor(f"out_{i}_dram", shape, _mybir.dt.float32, kind="ExternalOutput").ap())
    decoder_step(nc, *args)
    r = _run(nc, [arrays], core_ids=[0])
    return tuple(r.results[0][f"out_{i}_dram"] for i in range(len(_OUTS)))
```
